# Optimizing a Trainium2 kernel written in Bass

```python
import math
import jax, jax.numpy as jnp
from jax import lax
import numpy as np

D_MODEL = 1024
BATCH = 1
SEQ = 512
DEPTH = 1
DEC_BATCH = 8
DEC_SEQ = 4
PAST_LEN = 4096
PAGE_SIZE = 128

D_MIX = D_MODEL
D_MLSTM = D_MIX // 2
MH = 4
DH = D_MLSTM // MH
D_S5 = D_MIX // 4
S5_CH = 16
S5_G = D_S5 // S5_CH
S5_P = 64
D_CONV = D_MIX - D_MLSTM - D_S5
CONV_W = 3
D_FF = ((8 * D_MODEL // 3 + 127) // 128) * 128
CHUNK = 64
EPS = 1e-6
SPLIT_SIZES = (D_MLSTM, D_MLSTM, D_MLSTM, D_MLSTM, MH, MH, D_S5, D_CONV, D_CONV, D_CONV)
PROJ_W = sum(SPLIT_SIZES)

kernel_name = "hymba_style_mlstm_s5_shortconv_macaron"

def _rms(x):
    xf = x.astype(jnp.float32)
    return xf * lax.rsqrt(jnp.mean(xf * xf, axis=-1, keepdims=True) + EPS)

def rmsnorm(x, g):
    return (_rms(x) * g.astype(jnp.float32)).astype(x.dtype)

def swiglu(x, w1, w3, w2):
    return (jax.nn.silu(x @ w1) * (x @ w3)) @ w2

def mlstm_chunkwise(q, k, v, ig, fg, C0, n0, m0):
    f32 = jnp.float32
    Bb, S, H, Dh = q.shape
    L = CHUNK if S % CHUNK == 0 else S
    NC = S // L
    q = q.astype(f32)
    k = k.astype(f32) * (Dh ** -0.5)
    v = v.astype(f32)
    it_all = ig.astype(f32)
    lf_all = jax.nn.log_sigmoid(fg.astype(f32))

    def to_chunks(a):
        return a.reshape((Bb, NC, L) + a.shape[2:]).swapaxes(0, 1)

    mask = jnp.tril(jnp.ones((L, L), dtype=bool))

    def step(carry, inp):
        C, n, m = carry
        qc, kc, vc, ic, lfc = inp
        bt = jnp.cumsum(lfc, axis=1).transpose(0, 2, 1)
        it = ic.transpose(0, 2, 1)
        dmat = bt[..., :, None] - bt[..., None, :] + it[..., None, :]
        dmat = jnp.where(mask, dmat, -jnp.inf)
        inter = bt + m[..., None]
        mt = jnp.maximum(jnp.max(dmat, axis=-1), inter)
        w = jnp.exp(dmat - mt[..., None])
        s_inter = jnp.exp(inter - mt)
        sqk = jnp.einsum('bthd,bshd->bhts', qc, kc) * w
        num = (jnp.einsum('bhts,bshd->bthd', sqk, vc)
               + s_inter.transpose(0, 2, 1)[..., None] * jnp.einsum('bhvk,bthk->bthv', C, qc))
        den = jnp.sum(sqk, axis=-1) + s_inter * jnp.einsum('bhk,bthk->bht', n, qc)
        h = num / jnp.maximum(jnp.abs(den), jnp.exp(-mt)).transpose(0, 2, 1)[..., None]
        m_new = mt[..., -1]
        wk = jnp.exp(bt[..., -1:] - bt + it - m_new[..., None])
        decay = jnp.exp(bt[..., -1] + m - m_new)
        C_new = decay[..., None, None] * C + jnp.einsum('bhs,bshv,bshk->bhvk', wk, vc, kc)
        n_new = decay[..., None] * n + jnp.einsum('bhs,bshk->bhk', wk, kc)
        return (C_new, n_new, m_new), h

    carry, hs = lax.scan(step, (C0.astype(f32), n0.astype(f32), m0.astype(f32)),
                         (to_chunks(q), to_chunks(k), to_chunks(v), to_chunks(it_all), to_chunks(lf_all)))
    h = hs.swapaxes(0, 1).reshape(Bb, S, H, Dh)
    return h, carry

def s5_ssm(u, a_re, a_im, log_dt, b_re, b_im, c_re, c_im, d_skip, h0_re, h0_im):
    f32 = jnp.float32
    Bb, S, _ = u.shape
    uf = u.astype(f32).reshape(Bb, S, S5_G, S5_CH)
    dt = jnp.exp(log_dt.astype(f32))[:, None]
    lre = jnp.minimum(a_re.astype(f32), -1e-4)
    lim = a_im.astype(f32)
    mag = jnp.exp(lre * dt)
    ab_re = mag * jnp.cos(lim * dt)
    ab_im = mag * jnp.sin(lim * dt)
    den = lre * lre + lim * lim
    nr = ab_re - 1.0
    fre = (nr * lre + ab_im * lim) / den
    fim = (ab_im * lre - nr * lim) / den
    bu_re = jnp.einsum('bsgc,gpc->bsgp', uf, b_re.astype(f32))
    bu_im = jnp.einsum('bsgc,gpc->bsgp', uf, b_im.astype(f32))
    x_re = fre * bu_re - fim * bu_im
    x_im = fre * bu_im + fim * bu_re
    A_re = jnp.broadcast_to(ab_re, x_re.shape)
    A_im = jnp.broadcast_to(ab_im, x_re.shape)

    def combine(e1, e2):
        a1r, a1i, b1r, b1i = e1
        a2r, a2i, b2r, b2i = e2
        return (a2r * a1r - a2i * a1i, a2r * a1i + a2i * a1r,
                a2r * b1r - a2i * b1i + b2r, a2r * b1i + a2i * b1r + b2i)

    Pr, Pi, Hr, Hi = lax.associative_scan(combine, (A_re, A_im, x_re, x_im), axis=1)
    h0r = h0_re.astype(f32)[:, None]
    h0i = h0_im.astype(f32)[:, None]
    hr = Hr + Pr * h0r - Pi * h0i
    hi = Hi + Pr * h0i + Pi * h0r
    y = jnp.einsum('bsgp,gcp->bsgc', hr, c_re.astype(f32)) - jnp.einsum('bsgp,gcp->bsgc', hi, c_im.astype(f32))
    y = y.reshape(Bb, S, D_S5) + d_skip.astype(f32) * u.astype(f32)
    return y.astype(u.dtype), hr[:, -1], hi[:, -1]

def short_conv(z, w, buf):
    S = z.shape[1]
    zp = jnp.concatenate([buf.astype(z.dtype), z], axis=1)
    y = w[0] * zp[:, 0:S]
    for j in range(1, CONV_W):
        y = y + w[j] * zp[:, j:j + S]
    return y, zp[:, -(CONV_W - 1):]

def mixer(h, w_in, ig_bias, fg_bias, s5_a_re, s5_a_im, s5_log_dt, s5_b_re, s5_b_im, s5_c_re, s5_c_im,
          s5_d, w_glu, conv_w, mix_g, w_out, C0, n0, m0, sr0, si0, cb0):
    Bb, S, _ = h.shape
    proj = h @ w_in
    idx = [int(i) for i in np.cumsum(SPLIT_SIZES)[:-1]]
    q, k, v, o, ig, fg, u, bg, cg, hc = jnp.split(proj, idx, axis=-1)
    hm, (C1, n1, m1) = mlstm_chunkwise(q.reshape(Bb, S, MH, DH), k.reshape(Bb, S, MH, DH),
                                        v.reshape(Bb, S, MH, DH), ig + ig_bias, fg + fg_bias, C0, n0, m0)
    hm = jax.nn.sigmoid(o.astype(jnp.float32)).reshape(Bb, S, MH, DH) * hm
    out_a = _rms(hm).reshape(Bb, S, D_MLSTM)
    ys, sr1, si1 = s5_ssm(u, s5_a_re, s5_a_im, s5_log_dt, s5_b_re, s5_b_im, s5_c_re, s5_c_im, s5_d, sr0, si0)
    g = jax.nn.gelu(ys)
    out_b = _rms(g * jax.nn.sigmoid(g @ w_glu))
    yc, cb1 = short_conv(cg * hc, conv_w, cb0)
    out_c = _rms(bg * yc)
    cat = (jnp.concatenate([out_a, out_b, out_c], axis=-1) * mix_g.astype(jnp.float32)).astype(h.dtype)
    return cat @ w_out, (C1, n1, m1, sr1, si1, cb1)

def block(x, ffn1_w1, ffn1_w3, ffn1_w2, ffn2_w1, ffn2_w3, ffn2_w2, norm_g, w_in, ig_bias, fg_bias,
          s5_a_re, s5_a_im, s5_log_dt, s5_b_re, s5_b_im, s5_c_re, s5_c_im, s5_d, w_glu, conv_w, mix_g, w_out,
          C0, n0, m0, sr0, si0, cb0):
    x = x + 0.5 * rmsnorm(swiglu(rmsnorm(x, norm_g[0]), ffn1_w1, ffn1_w3, ffn1_w2), norm_g[1])
    mo, st = mixer(rmsnorm(x, norm_g[2]), w_in, ig_bias, fg_bias, s5_a_re, s5_a_im, s5_log_dt, s5_b_re, s5_b_im,
                   s5_c_re, s5_c_im, s5_d, w_glu, conv_w, mix_g, w_out, C0, n0, m0, sr0, si0, cb0)
    x = x + rmsnorm(mo, norm_g[3])
    x = x + 0.5 * rmsnorm(swiglu(rmsnorm(x, norm_g[4]), ffn2_w1, ffn2_w3, ffn2_w2), norm_g[5])
    return x, st

def run_trunk(x, C0, n0, m0, sr0, si0, cb0, weights):
    new = ([], [], [], [], [], [])
    for l in range(DEPTH):
        lw = [w[l] for w in weights]
        x, st = block(x, *lw, C0[l], n0[l], m0[l], sr0[l], si0[l], cb0[l])
        for lst, s in zip(new, st):
            lst.append(s)
    return x, [jnp.stack(s) for s in new]

def setup_inputs(seed: int = 0) -> dict:
    key = jax.random.key(seed)
    ks = jax.random.split(key, 32)
    f32 = jnp.float32
    nrm = lambda k, shp, s: jax.random.normal(k, shp, f32) * s
    L = DEPTH
    a_im = jnp.broadcast_to(jnp.pi * jnp.arange(S5_P, dtype=f32), (L, S5_G, S5_P))
    fg_base = jnp.broadcast_to(jnp.linspace(3.0, 6.0, MH, dtype=f32), (L, MH))
    return {
        "x_prompt": nrm(ks[0], (BATCH, SEQ, D_MODEL), 1.0),
        "x_sample": nrm(ks[1], (DEC_BATCH, DEC_SEQ, D_MODEL), 1.0),
        "state_mlstm_C": nrm(ks[2], (L, DEC_BATCH, MH, DH, DH), 0.1),
        "state_mlstm_n": nrm(ks[3], (L, DEC_BATCH, MH, DH), 0.1),
        "state_mlstm_m": nrm(ks[4], (L, DEC_BATCH, MH), 0.5),
        "state_s5_re": nrm(ks[5], (L, DEC_BATCH, S5_G, S5_P), 0.5),
        "state_s5_im": nrm(ks[6], (L, DEC_BATCH, S5_G, S5_P), 0.5),
        "state_conv": nrm(ks[7], (L, DEC_BATCH, CONV_W - 1, D_CONV), 1.0),
        "ffn1_w1": nrm(ks[8], (L, D_MODEL, D_FF), D_MODEL ** -0.5),
        "ffn1_w3": nrm(ks[9], (L, D_MODEL, D_FF), D_MODEL ** -0.5),
        "ffn1_w2": nrm(ks[10], (L, D_FF, D_MODEL), D_FF ** -0.5),
        "ffn2_w1": nrm(ks[11], (L, D_MODEL, D_FF), D_MODEL ** -0.5),
        "ffn2_w3": nrm(ks[12], (L, D_MODEL, D_FF), D_MODEL ** -0.5),
        "ffn2_w2": nrm(ks[13], (L, D_FF, D_MODEL), D_FF ** -0.5),
        "norm_g": 1.0 + nrm(ks[14], (L, 6, D_MODEL), 0.02),
        "w_in": nrm(ks[15], (L, D_MODEL, PROJ_W), D_MODEL ** -0.5),
        "ig_bias": nrm(ks[16], (L, MH), 0.1),
        "fg_bias": fg_base + nrm(ks[17], (L, MH), 0.1),
        "s5_a_re": -0.5 + nrm(ks[18], (L, S5_G, S5_P), 0.01),
        "s5_a_im": a_im + nrm(ks[19], (L, S5_G, S5_P), 0.01),
        "s5_log_dt": jax.random.uniform(ks[20], (L, S5_G), f32, math.log(0.001), math.log(0.1)),
        "s5_b_re": nrm(ks[21], (L, S5_G, S5_P, S5_CH), (2 * S5_CH) ** -0.5),
        "s5_b_im": nrm(ks[22], (L, S5_G, S5_P, S5_CH), (2 * S5_CH) ** -0.5),
        "s5_c_re": nrm(ks[23], (L, S5_G, S5_CH, S5_P), (2 * S5_P) ** -0.5),
        "s5_c_im": nrm(ks[24], (L, S5_G, S5_CH, S5_P), (2 * S5_P) ** -0.5),
        "s5_d": nrm(ks[25], (L, D_S5), 1.0),
        "w_glu": nrm(ks[26], (L, D_S5, D_S5), D_S5 ** -0.5),
        "conv_w": nrm(ks[27], (L, CONV_W, D_CONV), CONV_W ** -0.5),
        "mix_g": 1.0 + nrm(ks[28], (L, D_MIX), 0.02),
        "w_out": nrm(ks[29], (L, D_MIX, D_MODEL), D_MIX ** -0.5),
    }

def reference(x_prompt, x_sample, state_mlstm_C, state_mlstm_n, state_mlstm_m, state_s5_re, state_s5_im,
              state_conv, ffn1_w1, ffn1_w3, ffn1_w2, ffn2_w1, ffn2_w3, ffn2_w2, norm_g, w_in, ig_bias, fg_bias,
              s5_a_re, s5_a_im, s5_log_dt, s5_b_re, s5_b_im, s5_c_re, s5_c_im, s5_d, w_glu, conv_w, mix_g, w_out):
    weights = (ffn1_w1, ffn1_w3, ffn1_w2, ffn2_w1, ffn2_w3, ffn2_w2, norm_g, w_in, ig_bias, fg_bias,
               s5_a_re, s5_a_im, s5_log_dt, s5_b_re, s5_b_im, s5_c_re, s5_c_im, s5_d, w_glu, conv_w, mix_g, w_out)
    f32 = jnp.float32
    bp = x_prompt.shape[0]
    zC = jnp.zeros((DEPTH, bp, MH, DH, DH), f32)
    zn = jnp.zeros((DEPTH, bp, MH, DH), f32)
    zm = jnp.zeros((DEPTH, bp, MH), f32)
    zs = jnp.zeros((DEPTH, bp, S5_G, S5_P), f32)
    zc = jnp.zeros((DEPTH, bp, CONV_W - 1, D_CONV), x_prompt.dtype)
    y_prompt, p_st = run_trunk(x_prompt, zC, zn, zm, zs, zs, zc, weights)
    y_sample, s_st = run_trunk(x_sample, state_mlstm_C, state_mlstm_n, state_mlstm_m,
                               state_s5_re, state_s5_im, state_conv, weights)
    return (y_prompt, y_sample, p_st[0], p_st[1], p_st[2], p_st[3], p_st[4], p_st[5],
            s_st[0], s_st[1], s_st[2], s_st[3], s_st[4], s_st[5])


_drawn_inputs = setup_inputs


def setup_inputs(seed=0):
    import zlib

    import numpy as np

    out = dict(_drawn_inputs(seed))
    spreads = {}
    factors = {}
    for name, (base, spread) in spreads.items():
        noise = np.random.default_rng([zlib.crc32(name.encode()), seed]).standard_normal(out[name].shape)
        drawn = base * np.exp(spread * noise) if base else spread * noise
        out[name] = __import__('jax').numpy.asarray(drawn.astype(out[name].dtype))
    for name, factor in factors.items():
        out[name] = (out[name] * factor).astype(out[name].dtype)
    return out
```

```python
from contextlib import ExitStack

import numpy as np

import concourse.bass as bass
from concourse import mybir

F32 = mybir.dt.float32
F32R = mybir.dt.float32r
I32 = mybir.dt.int32
ALU = mybir.AluOpType
ACT = mybir.ActivationFunctionType

P = 128
D_MODEL, SEQ, DEC_BATCH, DEC_SEQ = 1024, 512, 8, 4
MH, DH, S5_G, S5_P, S5_CH, D_CONV, CONV_W = 4, 128, 16, 64, 16, 256, 3
D_FF = 2816
EPS = 1e-6
TS = DEC_BATCH * DEC_SEQ
T = SEQ + TS
HALF = T // 2
KD = D_MODEL // P
FT = D_FF // P
PARTS = (8, 8, 6)
assert sum(PARTS) == FT
UNIT = KD * P
NT = SEQ // P
NTT = NT + 1
LAST = T - P
SJ = S5_G * S5_P // P
CH = SEQ // 2
WBLK = [sum(SEQ - P * i for i in range(j)) for j in range(NT + 1)]
WCOL = WBLK[NT] + P
BIG = 3.0e38
MAGIC = 12582912.0

M_GATE, M_U, M_Q, M_K, M_V, M_CG, M_HC, M_BG, M_O, M_END = 0, 1, 3, 7, 11, 15, 17, 19, 21, 25
FFN_UNITS = 2 * FT + KD * len(PARTS)
MIX_BASE = FFN_UNITS
OUT_BASE = MIX_BASE + M_END
FFN2_BASE = OUT_BASE + KD

PRM = {}
_at = 0
for _n, _w in (("norm_g", 6 * KD), ("mix_g", KD), ("conv_w", CONV_W * 2), ("s5_d", 2), ("a_re", SJ), ("a_im", SJ),
               ("log_dt", SJ), ("gate_b", 2), ("m0", DEC_BATCH), ("h0", 2 * SJ * DEC_BATCH), ("conv0", 2 * DEC_BATCH * 2),
               ("n0", MH * DEC_BATCH), ("c_re", SJ * S5_CH), ("c_im", SJ * S5_CH), ("b_re", 2 * P), ("b_im", 2 * P), ("w_glu", 4 * P)):
    PRM[_n] = (_at, _at + _w)
    _at += _w
NPRM = _at
CST = {}
_at = 0
for _n, _w in (("ident", P), ("ones", 1), ("tri", P), ("bmask", P), ("batch", DEC_BATCH)):
    CST[_n] = (_at, _at + _w)
    _at += _w
NCST = _at
NCST2 = MH * P + CH
PI_BELOW = 3.1415925
INV_2PI = 0.15915494309189535
C1, C2, C3 = 6.28125, 0.0019350051879882812, 3.0199159819e-07
LN2_HI, LN2_LO, LOG2E = 0.693359375, -2.12194440e-4, 1.4426950408889634


def build(nc, A):
    with ExitStack() as ctx:
        place = [(nc.sbuf_base + 31) // 32 * 32]

        def sb(name, shape, dt=F32, at=None):
            n = int(np.prod(shape[1:])) * 4
            if at is None:
                at = place[0]
                place[0] += (n + 31) // 32 * 32
            return nc.alloc_sbuf_tensor_at(name, shape, dt, offset=at)

        def sem(name):
            return ctx.enter_context(nc.semaphore(name))

        ps = ctx.enter_context(nc.psum_tensor("ps", [P, 8, 512], F32))
        psf = ps[:].rearrange("p b c -> p (b c)")
        x = sb("x", [P, KD, T])
        xh = sb("xh", [P, KD, T], F32R)
        xl = sb("xl", [P, KD, T], F32R)
        raw = [sb(f"raw{i}", [P, UNIT]) for i in range(2)]
        wh = [sb(f"wh{i}", [P, UNIT], F32R) for i in range(2)]
        wl = [sb(f"wl{i}", [P, UNIT], F32R) for i in range(2)]
        act_t = sb("act_t", [P, 2, T])
        dve_t = sb("dve_t", [P, 2, T])
        y_at = place[0]
        y = sb("y", [P, KD, T])
        er_at = place[0]
        er = sb("er", [P, SJ, CH])
        ei = sb("ei", [P, SJ, CH])
        prm = sb("prm", [P, NPRM])
        cst = sb("cst", [P, NCST])
        gpost = sb("gpost", [P, 3, KD])
        stat = sb("stat", [P, 64])
        s5p = sb("s5p", [P, 18, SJ])
        cbd = sb("cbd", [P, 4, SJ, 32])
        arena_at = place[0]
        used = [0]

        def mix(name, *dims, alias=None, dt=F32):
            n = (int(np.prod(dims)) + 7) // 8 * 8
            if alias is None:
                alias = used[0]
                used[0] += n
            return sb(name, [P, *dims], dt, at=arena_at + 4 * alias)

        hh = sb("hh", [P, max(PARTS), T], F32R, at=arena_at)
        hl = sb("hl", [P, max(PARTS), T], F32R, at=arena_at + 4 * max(PARTS) * T)
        hid_end = 2 * max(PARTS) * T
        rot = mix("rot", 4, SEQ)
        prod = mix("prod", 4, SEQ)
        hst = mix("hst", 2, SEQ)
        ut = mix("ut", 2, T)
        wgt = sb("wgt", [P, MH, WCOL], at=arena_at)
        used[0] = max(used[0], MH * WCOL)
        vbig = mix("vbig", DEC_BATCH, P)
        q = mix("q", MH, T)
        k = mix("k", MH, T)
        V_AT = used[0]
        v = mix("v", MH, T)
        cg_at = arena_at + 4 * used[0]
        cg = mix("cg", 2, T)
        zp = mix("zp", 2, SEQ + 2)
        zs = mix("zs", 2, DEC_BATCH, DEC_SEQ + 2)
        gl = mix("gl", 2, T)
        mbc_at = arena_at + 4 * used[0]
        mbc = mix("mbc", MH, T)
        hs_at = arena_at + 4 * used[0]
        hs = mix("hs", 2, SJ, TS)
        used[0] += 8
        sbc = mix("sbc", MH, TS)
        cols = mix("cols", 60)
        hlast = mix("hlast", 2, SJ)
        s5o = mix("s5o", 2, SJ)
        s5so = mix("s5so", 2, SJ, DEC_BATCH)
        nst = mix("nst", MH, DEC_BATCH)
        v_at = arena_at + 4 * V_AT
        place[0] = arena_at + 4 * max(used[0], hid_end)
        assert place[0] <= nc.sbuf_usable_end, (place[0], nc.sbuf_usable_end)
        ang = sb("ang", [P, 5, CH], at=arena_at + 4 * hid_end)
        angd = sb("angd", [P, SJ, CH], at=arena_at + 4 * (hid_end + 5 * CH))
        cst2 = sb("cst2", [P, NCST2], at=cg_at)
        sel, tpos = cst2[:, 0:MH * P], cst2[:, MH * P:]
        acc = sb("acc", [P, T], at=mbc_at)
        pst = sb("pst", [P, MH, P + 1], at=hs_at)
        rows = sb("rows", [P, 8, T], at=y_at)
        kn = sb("kn", [P, MH, NT, P], at=y_at)
        sn = sb("sn", [P, 2, MH, P], at=y_at + 4 * 2048)
        vw = sb("vw", [P, 2, NT, P + 1], at=y_at + 4 * 3072)
        qs = sb("qs", [P, TS], at=y_at + 4 * 4104)
        prodn = sb("prodn", [P, P], at=y_at + 4 * 4136)
        wkm = sb("wkm", [P, MH, DEC_BATCH], at=y_at + 4 * 4264)
        vn = v[:, :, 0:SEQ].rearrange("p h (a d) -> p h a d", a=NT)
        bus = sb("bus", [P, 2, SJ, TS], at=v_at)
        xs5 = sb("xs5", [P, 2, SJ, TS], at=v_at + 4 * 512)
        tmp5 = sb("tmp5", [P, 4, SJ, TS], at=v_at + 4 * 1024)
        cs = sb("cs", [P, MH, DEC_BATCH, P], at=er_at)

        prm_ = {n: prm[:, a:b] for n, (a, b) in PRM.items()}
        cst_ = {n: cst[:, a:b] for n, (a, b) in CST.items()}
        ident, ones = cst_["ident"], cst_["ones"]
        norm_g = prm_["norm_g"].rearrange("p (n k) -> p n k", n=6)
        bbd = {"re": prm_["b_re"].rearrange("p (h s) -> p h s", h=2), "im": prm_["b_im"].rearrange("p (h s) -> p h s", h=2)}
        c_re = prm_["c_re"].rearrange("p (j c) -> p j c", j=SJ)
        c_im = prm_["c_im"].rearrange("p (j c) -> p j c", j=SJ)
        h0 = prm_["h0"].rearrange("p (r j b) -> p r j b", r=2, j=SJ)
        conv0 = prm_["conv0"].rearrange("p (c b w) -> p c b w", c=2, w=2)
        n0 = prm_["n0"].rearrange("p (h b) -> p h b", h=MH)
        m0 = prm_["m0"][0:MH, :]
        R_G, R_F, R_E, R_B, R_GM, R_M, R_KEEP, R_BND = range(8)
        LRE, DT, THETA, MAG, FF, FHI, FLO, IDEN, AR, AI, FRE, FIM, S0, S1, S2, S3, S4, S5 = range(18)

        def halves(t):
            return t.rearrange("p (a c) -> p a c", a=2)

        def pair(b):
            return ps[:, b:b + 2, 0:HALF]

        def row(r, a=0, b=T):
            return rows[0:MH, r, a:b]

        def starts(ap):
            return ap[:, SEQ:T:DEC_SEQ]

        raw_full = [sem(f"raw_full{i}") for i in range(2)]
        hi_done = sem("hi_done")
        split_done = sem("split_done")
        unit_used = sem("unit_used")
        xf_ready = sem("xf_ready")
        xh_ready = sem("xh_ready")
        xl_ready = sem("xl_ready")
        silu_ready = sem("silu_ready")
        h_ready = sem("h_ready")
        h_hi = sem("h_hi")
        h_lo = sem("h_lo")
        y_evac = sem("y_evac")
        ysq_ready = sem("ysq_ready")
        ysq_used = sem("ysq_used")
        xsq_ready = sem("xsq_ready")
        xsq_used = sem("xsq_used")
        x_new = sem("x_new")
        stat_done = sem("stat_done")
        var_ready = sem("var_ready")
        std_ready = sem("std_ready")
        rcol_ready = sem("rcol_ready")
        bc_done = sem("bc_done")
        prm_in = sem("prm_in")
        x_in = [sem(f"x_in{i}") for i in range(4)]
        cs_in = sem("cs_in")
        out_dma = sem("out_dma")
        m_out = sem("m_out")
        dve_chain = sem("dve_chain")
        pool_chain = sem("pool_chain")
        s5_par = sem("s5_par")
        ang_ready = sem("ang_ready")
        e_sin = sem("e_sin")
        e_ready = sem("e_ready")
        f_ready = sem("f_ready")
        t_evac = sem("t_evac")
        ga = sem("ga")
        gv = sem("gv")
        masks_ready = sem("masks_ready")
        bu_s = sem("bu_s")
        bus_evac = sem("bus_evac")
        hs_ready = sem("hs_ready")
        mb_done = sem("mb_done")
        mb_evac = sem("mb_evac")
        bu_done = sem("bu_done")
        rot_ready = sem("rot_ready")
        xrot_ready = sem("xrot_ready")
        prod_ready = sem("prod_ready")
        hst_ready = sem("hst_ready")
        ys_done = sem("ys_done")
        yss_done = sem("yss_done")
        ys_evac = sem("ys_evac")
        gelu_ready = sem("gelu_ready")
        glu_done = sem("glu_done")
        glu_sig = sem("glu_sig")
        outb_ready = sem("outb_ready")
        conv_used = sem("conv_used")
        outc_ready = sem("outc_ready")
        nat_done = sem("nat_done")
        nat_evac = sem("nat_evac")
        d_ready = sem("d_ready")
        w_exp = sem("w_exp")
        w_ready = sem("w_ready")
        sc_done = sem("sc_done")
        p_ready = sem("p_ready")
        qs_ready = sem("qs_ready")
        inter_done = sem("inter_done")
        vw_ready = sem("vw_ready")
        cdec_ready = sem("cdec_ready")
        cps_done = sem("cps_done")
        cps_used = sem("cps_used")
        num_done = sem("num_done")
        hso_ready = sem("hso_ready")
        st_done = sem("st_done")
        st_evac = sem("st_evac")
        s5_out = sem("s5_out")

        block = ctx.enter_context(nc.Block())
        OUTS_N = [0]

        @block.sync
        def _(spe):
            spe.dma_start(prm[:], A["prm"]).then_inc(prm_in, 16)
            for i in range(4):
                spe.dma_start(x[:, 2 * i:2 * i + 2], A["xT"][:, 2 * i:2 * i + 2]).then_inc(x_in[i], 16)
            spe.dma_start(cst[:], A["cst"]).then_inc(prm_in, 16)
            spe.dma_start(cst2[:], A["cst2"]).then_inc(prm_in, 16)

            def load(u, par, src, half_u, cols=UNIT):
                spe.wait_ge(split_done, u + 1)
                spe.dma_start(raw[par][:, 0:cols], src).then_inc(raw_full[par], 16)

            def ffn(f, u0):
                w13, w2 = A[f"w13_{f}"], A[f"w2_{f}"]
                k0 = 0
                for n in PARTS:
                    with spe.Fori(0, n) as i:
                        for c in range(2):
                            load(u0 + 2 * i + c, (u0 + c) % 2, w13[2 * k0 + 2 * i + c], None)
                    u0 += 2 * n
                    with spe.Fori(0, KD // 2) as i:
                        for c in range(2):
                            load(u0 + 2 * i + c, (u0 + c) % 2, w2[2 * i + c, :, k0 * P:(k0 + n) * P], None, n * P)
                    u0 += KD
                    k0 += n

            def store(dst, src):
                spe.dma_start(dst, src).then_inc(out_dma, 16)
                OUTS_N[0] += 1

            ffn(0, 0)
            for i in range(M_END):
                u = MIX_BASE + i
                load(u, u % 2, A["win"][i], None)
                if i == 9:
                    spe.wait_ge(gv, 13)
                    spe.dma_start(A["o_m"], row(R_E, SEQ - 1, T)).then_inc(m_out, 16)
                if i == 22:
                    spe.wait_ge(hst_ready, SJ)
                    spe.wait_ge(prod_ready, SJ)
                    spe.dma_start(cs[:], A["cT"]).then_inc(cs_in, 16)
                    spe.wait_ge(s5_out, 1)
                    store(A["o_ps5"], s5o[:])
                    store(A["o_ss5"], s5so[:])
                if i == 24:
                    spe.wait_ge(outc_ready, 2)
                    store(A["o_pconv"], zp[:, :, SEQ:SEQ + 2])
                    store(A["o_sconv"], zs[:, :, :, DEC_SEQ:DEC_SEQ + 2])
            load(OUT_BASE, OUT_BASE % 2, A["wout"][0], None)
            load(OUT_BASE + 1, (OUT_BASE + 1) % 2, A["wout"][1], None)
            for h in range(MH):
                spe.wait_ge(cps_used, 2 * h + 2)
                store(A["o_sC"][:, h], cs[:, h])
            spe.wait_ge(st_evac, MH)
            store(A["o_pC"], pst[:])
            store(A["o_sn"], nst[:])
            for m in range(2, KD):
                load(OUT_BASE + m, (OUT_BASE + m) % 2, A["wout"][m], None)
            ffn(1, FFN2_BASE)
            for kk in range(KD):
                spe.wait_ge(x_new, 2 * KD + kk + 1)
                store(A["o_yT"][:, kk], x[:, kk])
            spe.wait_ge(m_out, 16)
            spe.wait_ge(out_dma, 16 * OUTS_N[0])

        @block.scalar
        def _(act):
            cnt = {"norm": 0, "xs": 0, "ysq": 0, "e": 0, "sq": 0}

            def split(u, par, half, cols=UNIT):
                act.wait_ge(raw_full[par], 16 * (half + 1))
                act.wait_ge(unit_used, u + 1)
                nc.scalar.copy(wh[par][:, 0:cols], raw[par][:, 0:cols]).then_inc(hi_done, 1)

            def up_evac(hm, m, s, u_w3, mi):
                act.wait_ge(unit_used, u_w3 + 3)
                act.wait_ge(h_ready, hm + 1)
                nc.scalar.activation(halves(act_t[:, s]), pair(4 * s), ACT.Silu).then_inc(silu_ready, 1)
                act.wait_ge(h_ready, hm + 3)
                nc.scalar.copy(hh[:, mi, :], dve_t[:, s]).then_inc(h_hi, 1)

            def down_evac(m, s, yb, qb, last):
                if last:
                    act.wait_ge(y_evac, yb + m + 3)
                    act.wait_ge(ysq_used, qb + m + 1)
                    nc.scalar.activation(act_t[:, s], y[:, m, :], ACT.Square).then_inc(ysq_ready, 1)

            def angles(n):
                for _ in range(n):
                    j = cnt["e"]
                    cnt["e"] += 1
                    act.wait_ge(ang_ready, j + 1)
                    nc.scalar.activation(ei[:, j], angd[:, j], ACT.Sin, scale=2 * PI_BELOW).then_inc(e_sin, 1)
                    nc.scalar.activation(er[:, j], angd[:, j], ACT.Sin, scale=PI_BELOW).then_inc(e_sin, 1)
                    act.wait_ge(e_sin, 3 * j + 2)
                    nc.scalar.activation(er[:, j], er[:, j], ACT.Square).then_inc(e_sin, 1)

            def ffn(f, u0, hb, yb, qb, before):
                prev = before
                for p, n in enumerate(PARTS):
                    last = p == len(PARTS) - 1
                    if f == 0 and p:
                        angles(2)
                    half = lambda c: (u0 + c) // 2
                    split(u0, u0 % 2, half(0))
                    prev[0]()
                    split(u0 + 1, (u0 + 1) % 2, half(1))
                    prev[1]()
                    split(u0 + 2, u0 % 2, half(2))
                    split(u0 + 3, (u0 + 1) % 2, half(3))
                    up_evac(hb, 0, 0, u0 + 1, 0)
                    with act.Fori(1, n // 2) as i:
                        for c in range(4):
                            split(u0 + 4 * i + c, (u0 + c) % 2, (u0 + c) // 2 + 2 * i)
                            if c % 2:
                                mi = 2 * i - 1 + c // 2
                                up_evac(hb + mi, None, (c // 2 + 1) % 2, u0 + 2 * mi + 1, mi)
                    u1 = u0 + 2 * n
                    if f == 0:
                        angles((2, 1, 1)[p])
                    split(u1, u1 % 2, u1 // 2, n * P)
                    split(u1 + 1, (u1 + 1) % 2, (u1 + 1) // 2, n * P)
                    up_evac(hb + n - 1, None, 1, u1 - 1, n - 1)
                    with act.Fori(1, KD // 2) as i:
                        for c in range(2):
                            split(u1 + 2 * i + c, (u1 + c) % 2, (u1 + c) // 2 + i, n * P)
                            down_evac(2 * i - 2 + c, c, yb, qb, last)
                    prev = [lambda yb=yb, last=last: down_evac(6, 0, yb, qb, last),
                            lambda yb=yb, last=last: down_evac(7, 1, yb, qb, last)]
                    u0 = u1 + KD
                    hb += n
                    yb += KD
                return prev

            def root(w=NTT):
                n = cnt["norm"]
                cnt["norm"] += 1
                act.wait_ge(var_ready, n + 1)
                nc.scalar.activation(stat[:, 8:8 + w], stat[:, 0:w], ACT.Sqrt).then_inc(std_ready, 1)

            def square(src, wait):
                n = cnt["sq"]
                cnt["sq"] += 1
                wait()
                if n >= 2:
                    act.wait_ge(xsq_used, n - 1)
                nc.scalar.activation(act_t[:, n % 2], src, ACT.Square).then_inc(xsq_ready, 1)

            def hi_part(kk):
                e = cnt["xs"]
                cnt["xs"] += 1
                act.wait_ge(xf_ready, e + 1)
                nc.scalar.copy(xh[:, kk], dve_t[:, e % 2]).then_inc(xh_ready, 1)

            def pre_norm(n_x):
                for kk in range(KD):
                    if n_x is None:
                        square(x[:, kk], lambda: act.wait_ge(x_in[kk // 2], 16))
                    else:
                        square(x[:, kk], lambda: act.wait_ge(x_new, n_x + kk + 1))
                root()
                for kk in range(KD):
                    hi_part(kk)

            nothing = [lambda: None, lambda: None]
            pre_norm(None)
            tail = ffn(0, 0, 0, 0, 0, nothing)

            def mix_split(i):
                u = MIX_BASE + i
                split(u, u % 2, u // 2)

            mix_split(0)
            tail[0]()
            mix_split(1)
            tail[1]()
            root()
            pre_norm(0)

            def evac(i, dst, func=ACT.Copy, scale=1.0):
                act.wait_ge(unit_used, MIX_BASE + i + 3)
                b = 2 * (i % 2)
                nc.scalar.activation(halves(dst), pair(b), func, scale=scale).then_inc(t_evac, 1)

            def tile(i):
                if i == M_GATE:
                    act.wait_ge(unit_used, MIX_BASE + 3)
                    act.wait_ge(x_new, KD)
                    nc.scalar.activation(halves(row(R_G)), ps[0:MH, 0:2, 0:HALF], ACT.Identity,
                                         bias=prm_["gate_b"][0:MH, 0:1]).then_inc(ga, 1)
                    nc.scalar.copy(halves(row(R_F)), ps[32:32 + MH, 0:2, 0:HALF]).then_inc(ga, 1)
                    act.wait_ge(ga, 2)
                    nc.scalar.copy(stat[0:1, 63:64], stat[0:1, 0:1]).then_inc(t_evac, 1)
                elif i < M_Q:
                    evac(i, ut[:, i - M_U])
                elif i < M_K:
                    evac(i, q[:, i - M_Q])
                elif i < M_V:
                    evac(i, k[:, i - M_K], scale=DH ** -0.5)
                elif i < M_CG:
                    if i == M_V:
                        act.wait_ge(hs_ready, 1)
                    evac(i, v[:, i - M_V])
                elif i < M_HC:
                    evac(i, cg[:, i - M_CG])
                elif i < M_O:
                    n = i - M_HC
                    if n >= 2:
                        act.wait_ge(conv_used, n - 1)
                    evac(i, act_t[:, n % 2])
                else:
                    h = i - M_O
                    act.wait_ge(d_ready, MH)
                    evac(i, mbc[:, h], ACT.Sigmoid)

            def gates(s):
                if s == 3:
                    act.wait_ge(gv, 1)
                    nc.scalar.activation(row(R_E), row(R_F), ACT.Abs).then_inc(ga, 1)
                    act.wait_ge(ga, 3)
                    nc.scalar.activation(row(R_E), row(R_E), ACT.Exp, scale=-1.0).then_inc(ga, 1)
                if s == 4:
                    act.wait_ge(gv, 2)
                    nc.scalar.activation(row(R_E), row(R_E), ACT.Ln).then_inc(ga, 1)
                if s == 5:
                    act.wait_ge(gv, 13)
                    nc.scalar.activation(row(R_GM), row(R_GM), ACT.Exp).then_inc(ga, 1)
                    nc.scalar.activation(row(R_B), row(R_E), ACT.Exp, scale=-1.0).then_inc(ga, 1)
                    nc.scalar.activation(row(R_F, SEQ), row(R_F, SEQ), ACT.Exp).then_inc(ga, 1)

            def weights(h):
                act.wait_ge(d_ready, h + 1)
                nc.scalar.activation(wgt[:, h, 0:WBLK[NT]], wgt[:, h, 0:WBLK[NT]], ACT.Exp, scale=-1.0).then_inc(w_exp, 1)
                nc.scalar.activation(wgt[0:TS, h, WBLK[NT]:], wgt[0:TS, h, WBLK[NT]:], ACT.Exp, scale=-1.0).then_inc(w_exp, 1)

            def natural(h):
                if h == 0:
                    act.wait_ge(m_out, 16)
                act.wait_ge(nat_done, h + 1)
                nc.scalar.copy(kn[:, h], ps[:, 4, :].rearrange("p (a d) -> p a d", a=NT)).then_inc(nat_evac, 1)
                nc.scalar.copy(vn[:, h], ps[:, 5, :].rearrange("p (a d) -> p a d", a=NT)).then_inc(nat_evac, 1)

            for s in range(2, M_END + 2):
                if s < M_END:
                    mix_split(s)
                else:
                    u = OUT_BASE + s - M_END
                    split(u, u % 2, u // 2)
                tile(s - 2)
                gates(s)
                if s == 6:
                    act.wait_ge(bu_s, 1)
                    for g in range(4):
                        nc.scalar.copy(bus[:, :, g::4], ps[:, 4 + g, 0:4 * TS].rearrange("p (r j t) -> p r j t", r=2, t=TS))\
                            .then_inc(bus_evac, 1)
                if s == 8:
                    act.wait_ge(mb_done, 1)
                    nc.scalar.copy(mbc[:, :, 0:SEQ], ps[:, 4:8, :]).then_inc(mb_evac, 1)
                if s == 10:
                    act.wait_ge(mb_done, 2)
                    sv = ps[:, 4, 0:2 * MH * TS].rearrange("p (r h t) -> p r h t", r=2, h=MH)
                    nc.scalar.copy(mbc[:, :, SEQ:T], sv[:, 0]).then_inc(mb_evac, 1)
                    nc.scalar.copy(sbc[:], sv[:, 1]).then_inc(mb_evac, 1)
                    nc.scalar.copy(cols[:, 0:52], ps[:, 5, 0:52]).then_inc(mb_evac, 1)
                    nc.scalar.copy(cols[0:TS, 52:60], ps[0:TS, 5, 52:60]).then_inc(mb_evac, 1)
                if s == 22:
                    weights(0)
                    weights(1)
                if s == 23:
                    act.wait_ge(ys_evac, 1)
                    nc.scalar.activation(gl[:], gl[:], ACT.Gelu_apprx_tanh).then_inc(gelu_ready, 1)
                    weights(2)
                    weights(3)
                if s >= 23:
                    natural(s - 23)
            for m in range(2):
                act.wait_ge(glu_done, m + 1)
                act.wait_ge(conv_used, 4)
                nc.scalar.activation(halves(act_t[:, m]), pair(6 if m == 0 else 4), ACT.Sigmoid).then_inc(glu_sig, 1)
            act.wait_ge(nat_done, MH + 1)
            nc.scalar.copy(sn[0:TS, 0], ps[0:TS, 6, :].rearrange("p (h d) -> p h d", h=MH)).then_inc(nat_evac, 1)
            nc.scalar.copy(sn[0:TS, 1], ps[0:TS, 7, :].rearrange("p (h d) -> p h d", h=MH)).then_inc(nat_evac, 1)
            for c in range(2):
                square(cg[:, c], lambda: act.wait_ge(outb_ready, 2))
            root()
            for c in range(2):
                hi_part(c)
            for c in range(2):
                square(gl[:, c], lambda: None)
            root()
            for c in range(2):
                hi_part(2 + c)
            for h in range(MH + 1):
                if h >= 1:
                    root()
                    hi_part(3 + h)
                if h < MH:
                    square(mbc[:, h], lambda: act.wait_ge(hso_ready, h + 1))

            def out_sq(m):
                act.wait_ge(y_evac, 24 + m + 3)
                act.wait_ge(ysq_used, KD + m + 1)
                act.wait_ge(xsq_used, cnt["sq"])
                nc.scalar.activation(act_t[:, m % 2], y[:, m], ACT.Square).then_inc(ysq_ready, 1)

            for m in range(2, KD):
                u = OUT_BASE + m
                split(u, u % 2, u // 2)
                out_sq(m - 2)

            def before_ffn2():
                out_sq(7)
                root()
                pre_norm(KD)

            tail = ffn(1, FFN2_BASE, FT, 32, 2 * KD, [lambda: out_sq(6), before_ffn2])
            tail[0]()
            tail[1]()
            root()

        @block.vector
        def _(dve):
            V = nc.vector
            chain = [0]

            def link(ins):
                chain[0] += 1
                ins.then_inc(dve_chain, 1)
                dve.wait_ge(dve_chain, chain[0])

            def note(ins):
                chain[0] += 1
                ins.then_inc(dve_chain, 1)

            def settle():
                dve.wait_ge(dve_chain, chain[0])

            cnt = {"norm": 0, "xs": 0, "ysq": 0}

            def lo_part(u, par, cols=UNIT):
                dve.wait_ge(hi_done, u + 1)
                V.tensor_tensor(wl[par][:, 0:cols], raw[par][:, 0:cols], wh[par][:, 0:cols].bitcast(F32),
                                ALU.subtract).then_inc(split_done, 1)

            def up_evac(hm, s, u_w3, mi):
                dve.wait_ge(silu_ready, hm + 1)
                dve.wait_ge(unit_used, u_w3 + 3)
                V.tensor_tensor(halves(dve_t[:, s]), pair(4 * s + 2), halves(act_t[:, s]), ALU.mult).then_inc(h_ready, 1)
                dve.wait_ge(h_hi, hm + 1)
                V.tensor_tensor(hl[:, mi, :], dve_t[:, s], hh[:, mi, :].bitcast(F32), ALU.subtract).then_inc(h_lo, 1)

            def down_evac(m, s, yb, qb, u, p, last, banks):
                dve.wait_ge(unit_used, u + 3)
                if p == 0:
                    V.tensor_copy(halves(y[:, m, :]), pair(banks)).then_inc(y_evac, 1)
                else:
                    dve.wait_ge(y_evac, yb + m - KD + 3)
                    V.tensor_tensor(halves(y[:, m, :]), pair(banks), halves(y[:, m, :]), ALU.add).then_inc(y_evac, 1)
                if last:
                    dve.wait_ge(ysq_ready, qb + m + 1)
                    dve.wait_ge(ysq_used, qb + m + 2)
                    V.tensor_tensor(acc[:], acc[:], act_t[:, s], ALU.add).then_inc(ysq_used, 1)

            def ffn(f, u0, hb, yb, qb, before):
                prev = before
                for p, n in enumerate(PARTS):
                    last = p == len(PARTS) - 1
                    lo_part(u0, u0 % 2)
                    prev[0]()
                    lo_part(u0 + 1, (u0 + 1) % 2)
                    prev[1]()
                    lo_part(u0 + 2, u0 % 2)
                    lo_part(u0 + 3, (u0 + 1) % 2)
                    up_evac(hb, 0, u0 + 1, 0)
                    with dve.Fori(1, n // 2) as i:
                        for c in range(4):
                            lo_part(u0 + 4 * i + c, (u0 + c) % 2)
                            if c % 2:
                                mi = 2 * i - 1 + c // 2
                                up_evac(hb + mi, (c // 2 + 1) % 2, u0 + 2 * mi + 1, mi)
                    u1 = u0 + 2 * n
                    lo_part(u1, u1 % 2, n * P)
                    lo_part(u1 + 1, (u1 + 1) % 2, n * P)
                    up_evac(hb + n - 1, 1, u1 - 1, n - 1)
                    with dve.Fori(1, KD // 2) as i:
                        for c in range(2):
                            lo_part(u1 + 2 * i + c, (u1 + c) % 2, n * P)
                            m = 2 * i - 2 + c
                            down_evac(m, c, yb, qb, u1 + m, p, last, 2 * c)
                    prev = [lambda yb=yb, p=p, last=last, u1=u1: down_evac(6, 0, yb, qb, u1 + 6, p, last, 0),
                            lambda yb=yb, p=p, last=last, u1=u1: down_evac(7, 1, yb, qb, u1 + 7, p, last, 2)]
                    u0 = u1 + KD
                    hb += n
                    yb += KD
                return prev

            def scale_col(bank, width):
                n = cnt["norm"]
                cnt["norm"] += 1
                dve.wait_ge(stat_done, n + 1)
                V.tensor_scalar(stat[:, 0:NTT], ps[:, bank, 0:NTT], 1.0 / width, EPS, ALU.mult, ALU.add).then_inc(var_ready, 1)
                dve.wait_ge(std_ready, n + 1)
                V.reciprocal(stat[:, 16:16 + NTT], stat[:, 8:8 + NTT]).then_inc(rcol_ready, 1)
                dve.wait_ge(bc_done, n + 1)

            def lo_of(kk, e):
                dve.wait_ge(xh_ready, e + 1)
                V.tensor_tensor(xl[:, kk], dve_t[:, e % 2], xh[:, kk].bitcast(F32), ALU.subtract).then_inc(xl_ready, 1)

            def scaled(tiles):
                last = None
                for kk, write in tiles:
                    e = cnt["xs"]
                    cnt["xs"] += 1
                    if e >= 2:
                        dve.wait_ge(xh_ready, e - 1)
                        dve.wait_ge(xl_ready, e - 1)
                    write(dve_t[:, e % 2])
                    if last:
                        lo_of(*last)
                    last = (kk, e)
                lo_of(*last)

            def pre_norm(g):
                scale_col(3, D_MODEL)
                bc = psf[:, 6 * 512:6 * 512 + T]

                def write(kk):
                    return lambda out: V.scalar_tensor_tensor(out, x[:, kk], norm_g[:, g, kk:kk + 1], bc, ALU.mult,
                                                              ALU.mult).then_inc(xf_ready, 1)
                scaled([(kk, write(kk)) for kk in range(KD)])

            def post_norm(g):
                scale_col(6, D_MODEL)
                bc = psf[:, 4 * 512:4 * 512 + T]
                for kk in range(KD + 1):
                    if kk < KD:
                        note(V.tensor_tensor(y[:, kk], y[:, kk], bc, ALU.mult))
                        done = chain[0]
                    if kk:
                        dve.wait_ge(dve_chain, before)
                        V.scalar_tensor_tensor(x[:, kk - 1], y[:, kk - 1], gpost[:, g, kk - 1:kk], x[:, kk - 1],
                                               ALU.mult, ALU.add).then_inc(x_new, 1)
                    before = done

            V.memset(stat[:, 56:57], 0.0).then_inc(split_done, 2)
            V.memset(stat[:, 57:58], 0.0).then_inc(unit_used, 2)
            V.memset(stat[:, 58:59], 0.0).then_inc(h_ready, 2)
            V.memset(stat[:, 59:60], 0.0).then_inc(y_evac, 2)
            V.memset(stat[:, 60:61], 0.0).then_inc(ysq_used, 2)
            note(V.memset(acc[:], 0.0))
            note(V.memset(cbd[:], 0.0))
            note(V.memset(stat[:, 63:64], 0.0))

            def par(r):
                return s5p[:, r, :]

            def exp_to(out, src):
                link(V.tensor_scalar(par(S0), src, LOG2E, MAGIC, ALU.mult, ALU.add))
                link(V.tensor_scalar(par(S0), par(S0), -MAGIC, None, ALU.add))
                link(V.tensor_scalar(par(S0), par(S0), -126.0, 127.0, ALU.max, ALU.min))
                link(V.scalar_tensor_tensor(par(S1), par(S0), -LN2_HI, src, ALU.mult, ALU.add))
                link(V.scalar_tensor_tensor(par(S1), par(S0), -LN2_LO, par(S1), ALU.mult, ALU.add))
                link(V.tensor_scalar(par(S2), par(S1), 1.0 / 5040, None, ALU.mult))
                for c in (720, 120, 24, 6, 2, 1):
                    link(V.scalar_tensor_tensor(par(S2), par(S2), 1.0 / c, par(S1), ALU.add, ALU.mult))
                link(V.tensor_scalar(par(S3).bitcast(I32), par(S0), 127.0, 8388608.0, ALU.add, ALU.mult))
                link(V.scalar_tensor_tensor(out, par(S2), 1.0, par(S3), ALU.add, ALU.mult))

            def reduce(out, src, parts):
                link(V.scalar_tensor_tensor(out, par(S0), -parts[0], src, ALU.mult, ALU.add))
                for c in parts[1:]:
                    link(V.scalar_tensor_tensor(out, par(S0), -c, out, ALU.mult, ALU.add))

            dve.wait_ge(prm_in, 48)
            settle()
            a_im = prm_["a_im"]
            link(V.tensor_scalar(par(LRE), prm_["a_re"], -1e-4, None, ALU.min))
            exp_to(par(DT), prm_["log_dt"])
            link(V.tensor_tensor(par(THETA), a_im, par(DT), ALU.mult))
            link(V.tensor_tensor(par(S4), par(LRE), par(DT), ALU.mult))
            exp_to(par(MAG), par(S4))
            link(V.tensor_scalar(par(S0), par(THETA), INV_2PI, MAGIC, ALU.mult, ALU.add))
            link(V.tensor_scalar(par(S0), par(S0), -MAGIC, None, ALU.add))
            reduce(par(S4), par(THETA), (C1, C2, C3))
            link(V.tensor_scalar(par(FF), par(S4), INV_2PI, None, ALU.mult))
            link(V.tensor_scalar(par(S0), par(FF), 4096.0, MAGIC, ALU.mult, ALU.add))
            link(V.tensor_scalar(par(FHI), par(S0), -MAGIC, 1.0 / 4096, ALU.add, ALU.mult))
            link(V.tensor_copy(par(S0), par(FHI)))
            reduce(par(S5), par(S4), (C1, C2, C3))
            link(V.tensor_scalar(par(FLO), par(S5), INV_2PI, None, ALU.mult))
            link(V.tensor_tensor(par(S0), par(LRE), par(LRE), ALU.mult))
            link(V.tensor_tensor(par(S1), a_im, a_im, ALU.mult))
            link(V.tensor_tensor(par(S0), par(S0), par(S1), ALU.add))
            link(V.tensor_scalar(gpost[:, 0], norm_g[:, 1], 0.5, None, ALU.mult))
            link(V.tensor_scalar(gpost[:, 1], norm_g[:, 3], 1.0, None, ALU.mult))
            link(V.tensor_scalar(gpost[:, 2], norm_g[:, 5], 0.5, None, ALU.mult))
            V.reciprocal(par(IDEN), par(S0)).then_inc(s5_par, 1)

            pre_norm(0)
            tail = ffn(0, 0, 0, 0, 0, [lambda: None, lambda: None])
            lo_part(MIX_BASE, MIX_BASE % 2)
            tail[0]()
            lo_part(MIX_BASE + 1, (MIX_BASE + 1) % 2)
            tail[1]()
            post_norm(0)
            pre_norm(2)

            def gate(s):
                def step(ins):
                    gate.n += 1
                    ins.then_inc(gv, 1)
                    dve.wait_ge(gv, gate.n)
                if s == 2:
                    dve.wait_ge(ga, 2)
                    step(V.tensor_scalar(row(R_F), row(R_F), prm_["gate_b"][0:MH, 1:2], None, ALU.add))
                if s == 3:
                    dve.wait_ge(ga, 4)
                    step(V.tensor_scalar(row(R_E), row(R_E), 1.0, None, ALU.add))
                if s == 4:
                    dve.wait_ge(ga, 5)
                    dve.wait_ge(masks_ready, 4)
                    step(V.scalar_tensor_tensor(row(R_F), row(R_F), 0.0, row(R_E), ALU.min, ALU.subtract))
                    step(V.tensor_tensor_scan(row(R_B), row(R_KEEP), row(R_F), 0.0, ALU.mult, ALU.add))
                    step(V.tensor_tensor(row(R_G), row(R_G), row(R_B), ALU.subtract))
                    step(V.tensor_copy(row(R_GM), row(R_G)))
                    step(V.tensor_scalar(row(R_GM, 0, 1), row(R_GM, 0, 1), 0.0, None, ALU.max))
                    step(V.tensor_tensor(starts(row(R_GM)), starts(row(R_GM)), m0, ALU.max))
                    step(V.tensor_tensor_scan(row(R_M), row(R_BND), row(R_GM), 0.0, ALU.min, ALU.max))
                    step(V.tensor_scalar(row(R_GM, 0, SEQ), row(R_G, 0, SEQ), row(R_M, SEQ - 1, SEQ), None, ALU.subtract))
                    bt = lambda r: row(r, SEQ).rearrange("p (b t) -> p b t", b=DEC_BATCH)
                    step(V.tensor_tensor(bt(R_GM), bt(R_G), bt(R_M)[:, :, DEC_SEQ - 1:].to_broadcast([MH, DEC_BATCH, DEC_SEQ]),
                                         ALU.subtract))
                    step(V.tensor_tensor(row(R_E), row(R_B), row(R_M), ALU.add))
                    step(V.tensor_tensor(bt(R_F), m0.unsqueeze(2).to_broadcast([MH, DEC_BATCH, DEC_SEQ]), bt(R_M), ALU.subtract))
            gate.n = 0

            def s5_in(j):
                dve.wait_ge(bu_done, j + 1)
                e_re = er[:, j].unsqueeze(1).to_broadcast([P, 2, CH])
                e_im = ei[:, j].unsqueeze(1).to_broadcast([P, 2, CH])
                if j == 0:
                    dve.wait_ge(f_ready, 1)
                else:
                    dve.wait_ge(xrot_ready, 2 * j)
                two = lambda t: t.rearrange("p (a c) -> p a c", a=2)
                xr, xi = two(ps[:, 4, :]), two(ps[:, 5, :])
                for n, (a, b) in enumerate(((xr, e_re), (xi, e_im), (xi, e_re), (xr, e_im))):
                    V.tensor_tensor(two(rot[:, n]), a, b, ALU.mult).then_inc(rot_ready, 1)

            def s5_scan(j):
                mag = s5p[:, MAG, j:j + 1].to_broadcast([P, CH])
                e_r, e_i = er[:, j, CH - 1:CH], ei[:, j, CH - 1:CH]
                dve.wait_ge(xrot_ready, 2 * j + 2)
                gr, gi = rot[:, 0], rot[:, 2]
                note(V.tensor_tensor_scan(gr[:, 0:CH], mag, gr[:, 0:CH], 0.0, ALU.mult, ALU.add))
                note(V.tensor_tensor_scan(gi[:, 0:CH], mag, gi[:, 0:CH], 0.0, ALU.mult, ALU.add))
                settle()
                last_r, last_i = gr[:, CH - 1:CH], gi[:, CH - 1:CH]
                note(V.tensor_tensor(stat[:, 48:49], last_i, e_i, ALU.mult))
                note(V.tensor_tensor(stat[:, 49:50], last_r, e_i, ALU.mult))
                settle()
                note(V.scalar_tensor_tensor(stat[:, 50:51], last_r, e_r, stat[:, 48:49], ALU.mult, ALU.subtract))
                note(V.scalar_tensor_tensor(stat[:, 51:52], last_i, e_r, stat[:, 49:50], ALU.mult, ALU.add))
                settle()
                note(V.tensor_tensor_scan(gr[:, CH:], mag, gr[:, CH:], stat[:, 50:51], ALU.mult, ALU.add))
                note(V.tensor_tensor_scan(gi[:, CH:], mag, gi[:, CH:], stat[:, 51:52], ALU.mult, ALU.add))
                settle()
                e_re = er[:, j].unsqueeze(1).to_broadcast([P, 2, CH])
                e_im = ei[:, j].unsqueeze(1).to_broadcast([P, 2, CH])
                two = lambda t: t.rearrange("p (a c) -> p a c", a=2)
                if j:
                    dve.wait_ge(hst_ready, j)
                for n, (a, b) in enumerate(((gr, e_re), (gi, e_im), (gr, e_im), (gi, e_re))):
                    ins = V.tensor_tensor(two(prod[:, n]), two(a), b, ALU.mult)
                    chain[0] += 1
                    ins.then_inc(dve_chain, 1)
                settle()
                V.memset(stat[:, 52:53], 0.0).then_inc(prod_ready, 1)

            def exponents(h):
                if h == 0:
                    dve.wait_ge(hst_ready, SJ)
                    dve.wait_ge(mb_evac, 5)
                if h == 2:
                    dve.wait_ge(ys_done, SJ)
                for jb in range(NT):
                    note(V.tensor_scalar(wgt[:, h, WBLK[jb]:WBLK[jb + 1]], mbc[:, h, P * jb:SEQ],
                                         cols[:, 4 * jb + h:4 * jb + h + 1], 0.0, ALU.subtract, ALU.max))
                note(V.tensor_scalar(wgt[0:TS, h, WBLK[NT]:], mbc[0:TS, h, LAST:T], cols[0:TS, 52 + h:53 + h], 0.0,
                                     ALU.subtract, ALU.max))
                settle()
                V.memset(stat[:, 52:53], 0.0).then_inc(d_ready, 1)

            def conv_in(c):
                dve.wait_ge(t_evac, M_HC + c + 1)
                if c == 0:
                    note(V.memset(zp[:, :, 0:2], 0.0))
                    note(V.tensor_copy(zs[:, :, :, 0:2], conv0))
                note(V.tensor_tensor(zp[:, c, 2:], cg[:, c, 0:SEQ], act_t[:, c, 0:SEQ], ALU.mult))
                note(V.tensor_tensor(zs[:, c, :, 2:], cg[:, c, SEQ:].rearrange("p (b t) -> p b t", b=DEC_BATCH),
                                     act_t[:, c, SEQ:].rearrange("p (b t) -> p b t", b=DEC_BATCH), ALU.mult))
                settle()
                w = prm_["conv_w"].rearrange("p (w c) -> p w c", c=2)
                o_p = cg[:, c, 0:SEQ]
                o_s = cg[:, c, SEQ:].rearrange("p (b t) -> p b t", b=DEC_BATCH)
                note(V.tensor_scalar(o_p, zp[:, c, 0:SEQ], w[:, 0, c:c + 1], None, ALU.mult))
                note(V.tensor_scalar(o_s, zs[:, c, :, 0:DEC_SEQ], w[:, 0, c:c + 1], None, ALU.mult))
                for n in range(1, CONV_W):
                    settle()
                    note(V.scalar_tensor_tensor(o_p, zp[:, c, n:n + SEQ], w[:, n, c:c + 1], o_p, ALU.mult, ALU.add))
                    note(V.scalar_tensor_tensor(o_s, zs[:, c, :, n:n + DEC_SEQ], w[:, n, c:c + 1], o_s, ALU.mult, ALU.add))
                settle()
                V.memset(stat[:, 53:54], 0.0).then_inc(conv_used, 1)

            def conv_out(c):
                dve.wait_ge(t_evac, M_BG + c + 1)
                note(V.tensor_tensor(cg[:, c], cg[:, c], act_t[:, c], ALU.mult))
                settle()
                V.memset(stat[:, 53:54], 0.0).then_inc(conv_used, 1)
                V.memset(stat[:, 54:55], 0.0).then_inc(outc_ready, 1)

            for s in range(2, M_END + 2):
                u = MIX_BASE + s
                lo_part(u, u % 2)
                gate(s)
                if 12 <= s <= 19:
                    if s > 12:
                        s5_scan(s - 13)
                    s5_in(s - 12)
                if s == 20:
                    s5_scan(SJ - 1)
                if s == 21:
                    exponents(0)
                    exponents(1)
                if s == 22:
                    dve.wait_ge(ys_done, SJ)
                    dve.wait_ge(yss_done, 1)
                    for c in range(2):
                        d = prm_["s5_d"][:, c:c + 1]
                        note(V.scalar_tensor_tensor(gl[:, c, 0:SEQ], ut[:, c, 0:SEQ], d, ps[:, 6 + c, :], ALU.mult, ALU.add))
                        note(V.scalar_tensor_tensor(gl[:, c, SEQ:], ut[:, c, SEQ:], d, ps[:, 4, c * TS:(c + 1) * TS],
                                                    ALU.mult, ALU.add))
                    settle()
                    V.memset(stat[:, 52:53], 0.0).then_inc(ys_evac, 1)
                    exponents(2)
                    exponents(3)
                if s in (M_HC + 2, M_HC + 3):
                    conv_in(s - M_HC - 2)
                if s in (M_BG + 2, M_BG + 3):
                    conv_out(s - M_BG - 2)

            for m in range(2):
                dve.wait_ge(glu_sig, 2)
                V.tensor_tensor(gl[:, m], gl[:, m], act_t[:, m], ALU.mult).then_inc(outb_ready, 1)

            def cat_tile(src, kk, bank, g):
                def write(out):
                    V.scalar_tensor_tensor(out[:, 0:SEQ], src[:, 0:SEQ], g, ps[:, bank, :], ALU.mult, ALU.mult).then_inc(dve_chain, 1)
                    chain[0] += 1
                    V.scalar_tensor_tensor(out[:, SEQ:T], src[:, SEQ:T], g, ps[:, 6, 8:8 + TS], ALU.mult, ALU.mult)\
                     .then_inc(dve_chain, 1)
                    chain[0] += 1
                    settle()
                    V.memset(stat[:, 55:56], 0.0).then_inc(xf_ready, 1)
                return (kk, write)

            mix_g = prm_["mix_g"]
            scale_col(6, D_CONV)
            scaled([cat_tile(cg[:, c], c, 3, mix_g[:, c:c + 1]) for c in range(2)])
            scale_col(6, D_CONV)
            scaled([cat_tile(gl[:, c], 2 + c, 3, mix_g[:, 2 + c:3 + c]) for c in range(2)])

            def sample_q(h):
                if h == 0:
                    link(V.memset(prodn[:], 0.0))
                else:
                    dve.wait_ge(num_done, h)
                bt = lambda t: t.rearrange("p (b t) -> p b t", b=DEC_BATCH)
                link(V.tensor_tensor(qs[:], q[:, h, SEQ:], sbc[:, h], ALU.mult))
                V.tensor_tensor(bt(prodn[:, P - TS:]), bt(qs[:]), n0[:, h].unsqueeze(2).to_broadcast([P, DEC_BATCH, DEC_SEQ]),
                                ALU.mult).then_inc(qs_ready, 1)

            def add_memory(h, half):
                b0 = half * 4
                dve.wait_ge(cdec_ready, h + 1)
                dve.wait_ge(cps_done, 2 * h + half + 1)
                dst = cs[:, h, b0:b0 + 4]
                V.tensor_tensor(dst, ps[:, 7, :].rearrange("p (b d) -> p b d", b=4), dst, ALU.add).then_inc(cps_used, 1)

            sample_q(0)
            for h in range(MH + 1):
                if h < MH:
                    dve.wait_ge(sc_done, h + 1)
                    dve.wait_ge(w_ready, h + 1)
                    for a, b, c0 in ((0, 512, 0), (512, 896, 512), (896, WBLK[NT], 1024)):
                        note(V.tensor_tensor(wgt[:, h, a:b], psf[:, c0:c0 + b - a], wgt[:, h, a:b], ALU.mult))
                    note(V.tensor_tensor(wgt[0:TS, h, WBLK[NT]:], ps[0:TS, 1, 384:512], wgt[0:TS, h, WBLK[NT]:], ALU.mult))
                    settle()
                    V.memset(stat[:, 52:53], 0.0).then_inc(p_ready, 1)
                if h >= 1:
                    n = cnt["norm"]
                    cnt["norm"] += 1
                    dve.wait_ge(stat_done, n + 1)
                    link(V.tensor_tensor(stat[:, 0:NTT], ps[:, 6, 0:NTT], stat[:, 40:40 + NTT], ALU.mult))
                    V.tensor_scalar(stat[:, 0:NTT], stat[:, 0:NTT], 1.0 / DH, EPS, ALU.mult, ALU.add).then_inc(var_ready, 1)
                if h < MH:
                    add_memory(h, 0)
                if h >= 1:
                    dve.wait_ge(std_ready, n + 1)
                    link(V.reciprocal(stat[:, 8:8 + NTT], stat[:, 8:8 + NTT]))
                    V.tensor_tensor(stat[:, 16:16 + NTT], stat[:, 8:8 + NTT], stat[:, 32:32 + NTT], ALU.mult)\
                     .then_inc(rcol_ready, 1)
                if h < MH:
                    add_memory(h, 1)
                    dve.wait_ge(num_done, h + 1)
                    note(V.tensor_tensor(mbc[:, h, 0:SEQ], ps[:, 3 + h % 2, :], mbc[:, h, 0:SEQ], ALU.mult))
                    note(V.tensor_tensor(mbc[:, h, SEQ:], ps[:, 5, 0:TS], mbc[:, h, SEQ:], ALU.mult))
                    note(V.tensor_copy(stat[:, 24:24 + NTT], ps[:, 5, TS:TS + NTT]))
                    settle()
                    V.memset(stat[:, 52:53], 0.0).then_inc(hso_ready, 1)
                if h >= 1:
                    dve.wait_ge(bc_done, n + 1)
                    scaled([cat_tile(mbc[:, h - 1], 3 + h, 3 + (h - 1) % 2, mix_g[:, 3 + h:4 + h])])
                if h < MH:
                    link(V.scalar_tensor_tensor(stat[:, 24:24 + NTT], stat[:, 24:24 + NTT], -1.0, stat[:, 24:24 + NTT],
                                                ALU.mult, ALU.max))
                    link(V.tensor_tensor(stat[:, 24:24 + NTT], stat[:, 24:24 + NTT], cols[:, 32 + h:52:MH], ALU.max))
                    link(V.reciprocal(stat[:, 32:32 + NTT], stat[:, 24:24 + NTT]))
                    link(V.tensor_tensor(stat[:, 40:40 + NTT], stat[:, 32:32 + NTT], stat[:, 32:32 + NTT], ALU.mult))
                    dve.wait_ge(st_done, h + 1)
                    note(V.tensor_copy(pst[:, h], ps[:, 7, 0:P + 1]))
                    note(V.tensor_tensor(nst[:, h], n0[:, h], sbc[:, h, DEC_SEQ - 1::DEC_SEQ], ALU.mult))
                    settle()
                    link(V.tensor_tensor(nst[:, h], nst[:, h], ps[:, 7, P + 8:P + 8 + DEC_BATCH], ALU.add))
                    V.memset(stat[:, 52:53], 0.0).then_inc(st_evac, 1)
                    if h < MH - 1:
                        sample_q(h + 1)

            link(V.memset(acc[:], 0.0))
            def out_evac(m):
                dve.wait_ge(unit_used, OUT_BASE + m + 3)
                V.tensor_copy(halves(y[:, m]), pair(2 * (m % 2))).then_inc(y_evac, 1)
                dve.wait_ge(ysq_ready, KD + m + 1)
                dve.wait_ge(ysq_used, KD + m + 2)
                V.tensor_tensor(acc[:], acc[:], act_t[:, m % 2], ALU.add).then_inc(ysq_used, 1)

            for m in range(2, KD):
                u = OUT_BASE + m
                lo_part(u, u % 2)
                out_evac(m - 2)

            def before_ffn2():
                out_evac(7)
                post_norm(1)
                link(V.memset(acc[:], 0.0))
                pre_norm(4)

            tail = ffn(1, FFN2_BASE, FT, 32, 2 * KD, [lambda: out_evac(6), before_ffn2])
            tail[0]()
            tail[1]()
            post_norm(2)

        @block.gpsimd
        def _(pool):
            G = nc.gpsimd
            chain = [0]

            def link(ins):
                chain[0] += 1
                ins.then_inc(pool_chain, 1)
                pool.wait_ge(pool_chain, chain[0])

            def note(ins):
                chain[0] += 1
                ins.then_inc(pool_chain, 1)

            def settle():
                pool.wait_ge(pool_chain, chain[0])

            def signal(s_):
                settle()
                G.memset(stat[:, 61:62], 0.0).then_inc(s_, 1)

            def par(r):
                return s5p[:, r, :]

            def madd(out, src, a, b):
                return G.tensor_scalar(out, src, a, b, ALU.mult, ALU.add)

            pool.wait_ge(prm_in, 48)
            pool.wait_ge(s5_par, 1)
            tp = tpos
            for j in range(SJ):
                turns, whole, rest, small = (ang[:, n] for n in range(4))
                note(madd(turns, tp, s5p[:, FF, j:j + 1], MAGIC))
                note(madd(rest, tp, s5p[:, FHI, j:j + 1], 0.0))
                note(madd(small, tp, s5p[:, FLO, j:j + 1], 0.0))
                settle()
                link(G.tensor_scalar(whole, turns, -MAGIC, 1.0, ALU.add, ALU.mult))
                link(G.tensor_tensor(rest, rest, whole, ALU.subtract))
                link(G.tensor_tensor(rest, rest, small, ALU.add))
                link(madd(turns, rest, 1.0, MAGIC))
                link(G.tensor_scalar(whole, turns, -MAGIC, 1.0, ALU.add, ALU.mult))
                link(G.tensor_tensor(angd[:, j], rest, whole, ALU.subtract))
                signal(ang_ready)
            for j in range(SJ):
                pool.wait_ge(e_sin, 3 * j + 3)
                note(madd(er[:, j], er[:, j], -2.0, 1.0))
            settle()
            lim = prm_["a_im"]
            note(G.tensor_tensor(par(AR), par(MAG), er[:, :, 0], ALU.mult))
            note(G.tensor_tensor(par(AI), par(MAG), ei[:, :, 0], ALU.mult))
            settle()
            link(G.tensor_scalar(par(S0), par(AR), -1.0, 1.0, ALU.add, ALU.mult))
            note(G.tensor_tensor(par(S1), par(S0), par(LRE), ALU.mult))
            note(G.tensor_tensor(par(S2), par(AI), lim, ALU.mult))
            note(G.tensor_tensor(par(S3), par(AI), par(LRE), ALU.mult))
            note(G.tensor_tensor(par(S4), par(S0), lim, ALU.mult))
            settle()
            note(G.tensor_tensor(par(S1), par(S1), par(S2), ALU.add))
            note(G.tensor_tensor(par(S3), par(S3), par(S4), ALU.subtract))
            settle()
            note(G.tensor_tensor(par(FRE), par(S1), par(IDEN), ALU.mult))
            note(G.tensor_tensor(par(FIM), par(S3), par(IDEN), ALU.mult))
            settle()
            fr = par(FRE).unsqueeze(2).to_broadcast([P, SJ, S5_CH])
            fi = par(FIM).unsqueeze(2).to_broadcast([P, SJ, S5_CH])
            cf = [ang[:, n, 0:P].rearrange("p (j c) -> p j c", j=SJ) for n in range(5)]
            note(G.tensor_tensor(cf[0], c_re, fr, ALU.mult))
            note(G.tensor_tensor(cf[1], c_im, fi, ALU.mult))
            note(G.tensor_tensor(cf[2], c_re, fi, ALU.mult))
            note(G.tensor_tensor(cf[3], c_im, fr, ALU.mult))
            settle()
            link(G.tensor_tensor(cf[4], cf[2], cf[3], ALU.add))
            for g in range(2):
                a, c = slice(64 * g, 64 * g + 64), slice(S5_CH * g, S5_CH * (g + 1))
                note(G.tensor_tensor(cbd[a, 0, :, c], cf[0][a], cf[1][a], ALU.subtract))
                note(madd(cbd[a, 1, :, c], cf[4][a], -1.0, 0.0))
                note(madd(cbd[a, 2, :, c], c_re[a], 1.0, 0.0))
                note(madd(cbd[a, 3, :, c], c_im[a], -1.0, 0.0))
            signal(f_ready)

            pool.wait_ge(x_new, KD)
            note(G.memset(row(R_KEEP), 1.0))
            note(G.memset(row(R_BND), BIG))
            settle()
            G.memset(starts(row(R_KEEP)), 0.0).then_inc(masks_ready, 2)
            G.memset(starts(row(R_BND)), -BIG).then_inc(masks_ready, 2)

            pool.wait_ge(bus_evac, 4)
            big = lambda r, n: par(r).unsqueeze(2).to_broadcast([P, SJ, n])
            note(G.tensor_tensor(tmp5[:, 0], bus[:, 0], big(FRE, TS), ALU.mult))
            note(G.tensor_tensor(tmp5[:, 1], bus[:, 1], big(FIM, TS), ALU.mult))
            note(G.tensor_tensor(tmp5[:, 2], bus[:, 1], big(FRE, TS), ALU.mult))
            note(G.tensor_tensor(tmp5[:, 3], bus[:, 0], big(FIM, TS), ALU.mult))
            settle()
            note(G.tensor_tensor(xs5[:, 0], tmp5[:, 0], tmp5[:, 1], ALU.subtract))
            note(G.tensor_tensor(xs5[:, 1], tmp5[:, 2], tmp5[:, 3], ALU.add))
            settle()
            bt = lambda t: t.rearrange("p j (b t) -> p j b t", b=DEC_BATCH)
            now = [bt(hs[:, r]) for r in range(2)]
            inp = [bt(xs5[:, r]) for r in range(2)]
            t5 = [tmp5[:, n, :, 0:DEC_BATCH] for n in range(4)]
            for t in range(DEC_SEQ):
                hr, hi = (now[r][:, :, :, t - 1] if t else h0[:, r] for r in range(2))
                note(G.tensor_tensor(t5[0], hr, big(AR, DEC_BATCH), ALU.mult))
                note(G.tensor_tensor(t5[1], hi, big(AI, DEC_BATCH), ALU.mult))
                note(G.tensor_tensor(t5[2], hi, big(AR, DEC_BATCH), ALU.mult))
                note(G.tensor_tensor(t5[3], hr, big(AI, DEC_BATCH), ALU.mult))
                settle()
                note(G.tensor_tensor(t5[0], t5[0], t5[1], ALU.subtract))
                note(G.tensor_tensor(t5[2], t5[2], t5[3], ALU.add))
                settle()
                note(G.tensor_tensor(now[0][:, :, :, t], t5[0], inp[0][:, :, :, t], ALU.add))
                note(G.tensor_tensor(now[1][:, :, :, t], t5[2], inp[1][:, :, :, t], ALU.add))
                settle()
            signal(hs_ready)

            for j in range(SJ):
                pool.wait_ge(rot_ready, 4 * j + 4)
                G.tensor_tensor(rot[:, 0], rot[:, 0], rot[:, 1], ALU.add).then_inc(xrot_ready, 1)
                G.tensor_tensor(rot[:, 2], rot[:, 2], rot[:, 3], ALU.subtract).then_inc(xrot_ready, 1)
                pool.wait_ge(prod_ready, j + 1)
                if j:
                    pool.wait_ge(ys_done, j)
                note(G.tensor_tensor(hst[:, 0], prod[:, 0], prod[:, 1], ALU.subtract))
                note(G.tensor_tensor(hst[:, 1], prod[:, 2], prod[:, 3], ALU.add))
                settle()
                link(madd(hlast[:, :, j:j + 1], hst[:, :, SEQ - 1:SEQ], 1.0, 0.0))
                G.memset(stat[:, 61:62], 0.0).then_inc(hst_ready, 1)
            hr, hi = hlast[:, 0], hlast[:, 1]
            note(G.tensor_tensor(par(S0), hr, par(FRE), ALU.mult))
            note(G.tensor_tensor(par(S1), hi, par(FIM), ALU.mult))
            note(G.tensor_tensor(par(S2), hi, par(FRE), ALU.mult))
            note(G.tensor_tensor(par(S3), hr, par(FIM), ALU.mult))
            settle()
            note(G.tensor_tensor(s5o[:, 0], par(S0), par(S1), ALU.subtract))
            note(G.tensor_tensor(s5o[:, 1], par(S2), par(S3), ALU.add))
            for r in range(2):
                note(madd(s5so[:, r], now[r][:, :, :, DEC_SEQ - 1], 1.0, 0.0))
            signal(s5_out)

            for h in range(MH):
                note(madd(wkm[0:TS, h], cst_["batch"][0:TS], cols[0:TS, 56 + h:57 + h], 0.0))
            for h in range(MH):
                pool.wait_ge(w_exp, 2 * h + 2)
                for jb in range(NT):
                    w = wgt[:, h, WBLK[jb]:WBLK[jb] + P]
                    note(G.tensor_tensor(w, w, cst_["tri"], ALU.mult))
                w = wgt[0:TS, h, WBLK[NT]:]
                note(G.tensor_tensor(w, w, cst_["bmask"][0:TS], ALU.mult))
                signal(w_ready)
            for h in range(MH):
                pool.wait_ge(nat_evac, 2 * MH + 2)
                if h >= 2:
                    pool.wait_ge(st_done, h - 1)
                for a in range(NT):
                    note(madd(vw[:, h % 2, a, 0:P], vn[:, h, a], cols[:, 16 + 4 * a + h:17 + 4 * a + h], 0.0))
                note(madd(vw[:, h % 2, :, P], cols[:, 16 + h:32:MH], 1.0, 0.0))
                if h:
                    pool.wait_ge(cps_done, 2 * h)
                note(G.tensor_tensor(vbig[0:TS], sn[0:TS, 1, h].unsqueeze(1).to_broadcast([TS, DEC_BATCH, P]),
                                     wkm[0:TS, h].unsqueeze(2).to_broadcast([TS, DEC_BATCH, P]), ALU.mult))
                signal(vw_ready)
                pool.wait_ge(inter_done, h + 1)
                note(G.tensor_tensor(cs[:, h], cs[:, h],
                                     sbc[:, h, DEC_SEQ - 1::DEC_SEQ].unsqueeze(2).to_broadcast([P, DEC_BATCH, P]), ALU.mult))
                signal(cdec_ready)

        @block.tensor
        def _(pe):
            mm = nc.tensor.matmul
            cnt = {"norm": 0, "sq": 0, "post": 0}

            def unit(par, bank, n, a_hi, a_lo, wait_k=None):
                for kk in range(n):
                    if wait_k:
                        wait_k(kk)
                    for i, (w, a) in enumerate(((wh, a_hi), (wh, a_lo), (wl, a_hi))):
                        for s in range(2):
                            last = mm(ps[:, bank + s, 0:HALF], w[par][:, kk * P:(kk + 1) * P],
                                      a[:, kk, s * HALF:(s + 1) * HALF], start=(kk == 0 and i == 0),
                                      stop=(kk == n - 1 and i == 2))
                last.then_inc(unit_used, 1)

            def ffn(u0, hb, yb, e0):
                for p, n in enumerate(PARTS):
                    with pe.Fori(0, n // 2) as i:
                        for c in range(4):
                            par, s = (u0 + c) % 2, c // 2
                            pe.wait_ge(split_done, u0 + 4 * i + c + 3)
                            if c % 2 == 0:
                                pe.wait_ge(h_ready, hb + 2 * i + s + 1)
                            if s == 0 and p:
                                pe.wait_ge(y_evac, yb + 1 + c)
                            first = p == 0 and c == 0
                            unit(par, 2 * c, KD, xh, xl, (lambda kk: pe.wait_ge(xl_ready, e0 + kk + 1)) if first else None)
                    u0 += 2 * n
                    with pe.Fori(0, KD // 2) as i:
                        for c in range(2):
                            pe.wait_ge(split_done, u0 + 2 * i + c + 3)
                            pe.wait_ge(y_evac, yb + 2 * i + c + 1)
                            unit((u0 + c) % 2, 2 * c, n, hh, hl,
                                 (lambda kk: pe.wait_ge(h_lo, hb + kk + 1)) if c == 0 else None)
                    u0 += KD
                    hb += n
                    yb += KD

            def token_sums(src, bank, first, last):
                for c in range(NTT):
                    lo = P * c if c < NT else LAST
                    ins = mm(ps[:, bank, c:c + 1], src[:, lo:lo + P], ones, start=(first and c == 0), stop=last,
                             skip_group_check=True)
                return ins

            def squares(n, bank):
                for i in range(n):
                    pe.wait_ge(xsq_ready, cnt["sq"] + 1)
                    ins = token_sums(act_t[:, cnt["sq"] % 2], bank, i == 0, i == n - 1)
                    cnt["sq"] += 1
                    ins.then_inc(xsq_used, 1)
                mm(ps[:, bank, NTT:NTT + 1], ident, ones, start=False, stop=True, skip_group_check=True).then_inc(stat_done, 1)

            def spread(bank, bank_s, col_s):
                n = cnt["norm"]
                cnt["norm"] += 1
                pe.wait_ge(rcol_ready, n + 1)
                for c in range(NTT):
                    w = P if c < NT else TS
                    out = ps[:, bank, P * c:P * c + P] if c < NT else ps[:, bank_s, col_s:col_s + TS]
                    ins = mm(out, stat[:, 16 + c:17 + c].to_broadcast([P, P]), ident[:, P - w:P], start=True, stop=True)
                ins.then_inc(bc_done, 1)

            def pre_norm():
                squares(KD, 3)
                spread(6, 7, 0)

            def post_norm():
                cnt["post"] += KD
                pe.wait_ge(ysq_used, cnt["post"] + 2)
                token_sums(acc, 6, True, True).then_inc(stat_done, 1)
                spread(4, 5, 0)

            pe.wait_ge(prm_in, 48)
            pre_norm()
            ffn(0, 0, 0, 0)
            post_norm()
            pre_norm()

            def gate_spread():
                pe.wait_ge(gv, 13)
                pe.wait_ge(ga, 8)
                pe.wait_ge(bus_evac, 4)
                for h in range(MH):
                    ins = mm(ps[:, 4 + h, :], sel[0:MH, h * P:(h + 1) * P], row(R_M, 0, SEQ), start=True, stop=True)
                ins.then_inc(mb_done, 1)

            def gate_turn():
                pe.wait_ge(mb_evac, 1)
                for r, src in enumerate((R_M, R_F)):
                    for h in range(MH):
                        at = (r * MH + h) * TS
                        mm(ps[:, 4, at:at + TS], sel[0:MH, h * P:(h + 1) * P], row(src, SEQ), start=True, stop=True)
                i4 = ident[0:MH, 0:MH]
                for n, r in enumerate((R_G, R_GM)):
                    for a in range(NT):
                        nc.tensor.transpose(ps[:, 5, 16 * n + 4 * a:16 * n + 4 * a + 4], row(r, P * a, P * a + P), i4)
                    nc.tensor.transpose(ps[0:TS, 5, 52 + 4 * n:56 + 4 * n], row(r, SEQ), i4)
                for a in range(NTT):
                    lo = P * a if a < NT else LAST
                    ins = nc.tensor.transpose(ps[:, 5, 32 + 4 * a:36 + 4 * a], row(R_B, lo, lo + P), i4)
                ins.then_inc(mb_done, 1)

            def sample_bu():
                pe.wait_ge(t_evac, M_U + 2)
                for r, mat in enumerate(("re", "im")):
                    for j in range(SJ):
                        a = slice(32 * (j % 4), 32 * (j % 4) + 32)
                        at = (2 * r + j // 4) * TS
                        ins = mm(ps[:, 4 + j % 4, at:at + TS], bbd[mat][a, j // 4, :], ut[a, j // 4, SEQ:], start=True, stop=True)
                ins.then_inc(bu_s, 1)

            def bu(j):
                if j == 0:
                    pe.wait_ge(mb_evac, 5)
                else:
                    pe.wait_ge(rot_ready, 4 * j)
                a = slice(32 * (j % 4), 32 * (j % 4) + 32)
                for bank, mat in ((4, "re"), (5, "im")):
                    ins = mm(ps[:, bank, :], bbd[mat][a, j // 4, :], ut[a, j // 4, 0:SEQ], start=True, stop=True)
                ins.then_inc(bu_done, 1)

            def s5_y(j):
                pe.wait_ge(hst_ready, j + 1)
                a = slice(32 * (j % 4), 32 * (j % 4) + 32)
                for r in range(2):
                    ins = mm(ps[a, 6 + j // 4, :], cbd[:, r, j, :], hst[:, r], start=(r == 0), stop=(r == 1))
                ins.then_inc(ys_done, 1)

            def s5_y_sample():
                pe.wait_ge(hs_ready, 1)
                pe.wait_ge(rot_ready, 4 * SJ)
                for j in range(SJ):
                    a = slice(32 * (j % 4), 32 * (j % 4) + 32)
                    for r in range(2):
                        ins = mm(ps[a, 4, (j // 4) * TS:(j // 4 + 1) * TS], cbd[:, 2 + r, j, :], hs[:, r, j],
                                 start=(r == 0), stop=(r == 1))
                ins.then_inc(yss_done, 1)

            def turn(h):
                pe.wait_ge(ys_evac, 1)
                if h:
                    pe.wait_ge(nat_evac, 2 * h)
                for a in range(NT):
                    nc.tensor.transpose(ps[:, 4, a * P:(a + 1) * P], k[:, h, a * P:(a + 1) * P], ident)
                for a in range(NT):
                    ins = nc.tensor.transpose(ps[:, 5, a * P:(a + 1) * P], v[:, h, a * P:(a + 1) * P], ident)
                ins.then_inc(nat_done, 1)

            after = {4: [sample_bu], 6: [gate_spread], 8: [gate_turn], 21: [lambda: s5_y_sample()],
                     22: [lambda: turn(0)], 23: [lambda: turn(1)], 24: [lambda: turn(2)]}
            for j in range(SJ):
                after.setdefault(10 + j, []).append(lambda j=j: bu(j))
                after.setdefault(13 + j, []).append(lambda j=j: s5_y(j))
            for i in range(M_END):
                u = MIX_BASE + i
                pe.wait_ge(split_done, u + 3)
                if i >= 2:
                    pe.wait_ge(t_evac, i - 1)
                unit(u % 2, 2 * (i % 2), KD, xh, xl, (lambda kk: pe.wait_ge(xl_ready, KD + kk + 1)) if i == 0 else None)
                for f in after.get(i, ()):
                    f()

            pe.wait_ge(gelu_ready, 1)
            for m in range(2):
                if m == 1:
                    turn(3)
                    pe.wait_ge(nat_evac, 2 * MH)
                bank = 6 if m == 0 else 4
                wg = prm_["w_glu"].rearrange("p (k c) -> p k c", k=2)
                for kk in range(2):
                    for s in range(2):
                        ins = mm(ps[:, bank + s, 0:HALF], wg[:, kk, m * P:(m + 1) * P], gl[:, kk, s * HALF:(s + 1) * HALF],
                                 start=(kk == 0), stop=(kk == 1))
                ins.then_inc(glu_done, 1)
            pe.wait_ge(glu_sig, 1)
            for h in range(MH):
                nc.tensor.transpose(ps[0:TS, 6, h * P:(h + 1) * P], k[:, h, SEQ:], ident)
            for h in range(MH):
                ins = nc.tensor.transpose(ps[0:TS, 7, h * P:(h + 1) * P], v[:, h, SEQ:], ident)
            ins.then_inc(nat_done, 1)

            pe.wait_ge(nat_evac, 2 * MH + 2)
            squares(2, 6)
            spread(3, 6, 8)
            pe.wait_ge(xf_ready, 2 * KD + 2)
            squares(2, 6)
            spread(3, 6, 8)

            pe.wait_ge(t_evac, M_END)
            pe.wait_ge(glu_sig, 2)
            pe.wait_ge(cs_in, 16)
            for h in range(MH + 1):
                if h < MH:
                    if h:
                        pe.wait_ge(p_ready, h)
                    for jb in range(NT):
                        at = (0, 512, 1024, 1280)[jb]
                        mm(psf[:, at:at + SEQ - P * jb], k[:, h, P * jb:P * jb + P], q[:, h, P * jb:SEQ], start=True, stop=True)
                    mm(ps[0:TS, 1, 384:512], k[:, h, SEQ:], q[:, h, LAST:T], start=True, stop=True).then_inc(sc_done, 1)
                    pe.wait_ge(hso_ready, h)
                    pe.wait_ge(qs_ready, h + 1)
                    for b in range(DEC_BATCH):
                        c = slice(b * DEC_SEQ, (b + 1) * DEC_SEQ)
                        ins = mm(ps[:, 5, c], cs[:, h, b], qs[:, c], start=(b == 0), stop=False, skip_group_check=True)
                    ins.then_inc(inter_done, 1)
                    pe.wait_ge(st_evac, h)
                    pe.wait_ge(vw_ready, h + 1)
                    mm(ps[:, 7, :], sn[0:TS, 0, h], vbig[0:TS, 0:4].rearrange("p b d -> p (b d)"), start=True, stop=True)\
                        .then_inc(cps_done, 1)
                if h:
                    pe.wait_ge(xf_ready, 2 * KD + 4 + h - 1)
                    squares(1, 6)
                if h < MH:
                    pe.wait_ge(cps_used, 2 * h + 1)
                    mm(ps[:, 7, :], sn[0:TS, 0, h], vbig[0:TS, 4:8].rearrange("p b d -> p (b d)"), start=True, stop=True)\
                        .then_inc(cps_done, 1)
                    pe.wait_ge(p_ready, h + 1)
                    pe.wait_ge(xf_ready, 2 * KD + 4 + max(h - 1, 0))
                    for jb in range(NT):
                        mm(ps[:, 3 + h % 2, P * jb:], vn[:, h, jb], wgt[:, h, WBLK[jb]:WBLK[jb + 1]], start=(jb == 0),
                           stop=(jb == NT - 1), skip_group_check=True)
                    own = wgt[0:TS, h, WBLK[NT]:]
                    mm(ps[:, 5, 0:TS], sn[0:TS, 1, h], own[:, P - TS:], start=False, stop=True, skip_group_check=True)
                    for a in range(NT):
                        for jb in range(a + 1):
                            at = WBLK[jb] + P * (a - jb)
                            mm(ps[:, 5, TS + a:TS + a + 1], wgt[:, h, at:at + P], ones, start=False, stop=(jb == a),
                               skip_group_check=True)
                    mm(ps[:, 5, TS + NT:TS + NTT], own, ones[0:TS], start=False, stop=False, skip_group_check=True)
                    mm(ps[:, 5, TS + NT:TS + NTT], prodn[:], ones, start=False, stop=True, skip_group_check=True)\
                        .then_inc(num_done, 1)
                if h:
                    spread(3 + (h - 1) % 2, 6, 8)
                if h < MH:
                    pe.wait_ge(cps_used, 2 * h + 2)
                    for a in range(NT):
                        mm(ps[:, 7, 0:P + 1], kn[:, h, a], vw[:, h % 2, a], start=(a == 0), stop=(a == NT - 1))
                    mm(ps[:, 7, P + 8:P + 8 + DEC_BATCH], sn[0:TS, 0, h], wkm[0:TS, h], start=True, stop=True)\
                        .then_inc(st_done, 1)

            for m in range(KD):
                u = OUT_BASE + m
                pe.wait_ge(split_done, u + 3)
                if m == 0:
                    pe.wait_ge(xf_ready, 3 * KD)
                pe.wait_ge(y_evac, 24 + m + 1)
                unit(u % 2, 2 * (m % 2), KD, xh, xl, (lambda kk: pe.wait_ge(xl_ready, 2 * KD + kk + 1)) if m == 0 else None)
            post_norm()
            pre_norm()
            ffn(FFN2_BASE, FT, 32, 3 * KD)
            post_norm()


def _tiles(w, rows, cols):
    return w.reshape(rows, P, cols, P).transpose(2, 1, 0, 3).reshape(cols, P, rows * P)


def _features(a):
    n = a.shape[-1] // P
    a = a.reshape(a.shape[:-1] + (n, P))
    return np.moveaxis(np.moveaxis(a, -1, 0), -1, 1)


_OUTS = {
    "o_yT": (P, KD, T), "o_pC": (P, MH, P + 1), "o_m": (MH, 1 + TS), "o_ps5": (P, 2, SJ), "o_pconv": (P, 2, 2),
    "o_sC": (P, MH, DEC_BATCH, P), "o_sn": (P, MH, DEC_BATCH), "o_ss5": (P, 2, SJ, DEC_BATCH),
    "o_sconv": (P, 2, DEC_BATCH, 2),
}


def _constants():
    c = np.zeros((P, NCST), np.float32)
    put = lambda n, a: c.__setitem__((slice(0, a.shape[0]), slice(*CST[n])), a)
    put("ident", np.eye(P, dtype=np.float32))
    put("ones", np.ones((P, 1), np.float32))
    put("tri", np.triu(np.ones((P, P), np.float32)))
    bm = np.zeros((TS, P), np.float32)
    for b in range(DEC_BATCH):
        a = b * DEC_SEQ
        bm[a:a + DEC_SEQ, P - TS + a:P - TS + a + DEC_SEQ] = np.triu(np.ones((DEC_SEQ, DEC_SEQ), np.float32))
    put("bmask", bm)
    put("batch", np.repeat(np.eye(DEC_BATCH, dtype=np.float32), DEC_SEQ, axis=0))
    c2 = np.zeros((P, NCST2), np.float32)
    c2[0:MH, 0:MH * P] = np.repeat(np.eye(MH, dtype=np.float32), P, axis=1)
    c2[:, MH * P:] = np.arange(1, CH + 1, dtype=np.float32)
    return c, c2


def _layout(i):
    g = lambda n: np.asarray(i[n])[0]
    out = {}
    xs = np.concatenate([np.asarray(i["x_prompt"])[0], np.asarray(i["x_sample"]).reshape(TS, D_MODEL)])
    out["xT"] = _features(xs)
    for f in range(2):
        w1, w3, w2 = (g(f"ffn{f + 1}_{w}") for w in ("w1", "w3", "w2"))
        out[f"w13_{f}"] = np.stack([_tiles(w1, KD, FT), _tiles(w3, KD, FT)], axis=1).reshape(2 * FT, P, UNIT)
        out[f"w2_{f}"] = _tiles(w2, FT, KD)
    w = g("w_in")
    dm = MH * DH
    at = np.cumsum([0, dm, dm, dm, dm, MH, MH, 256, 256, 256, 256])
    q_, k_, v_, o_, i_, f_, u_, b_, c_, h_ = (w[:, a:b] for a, b in zip(at[:-1], at[1:]))
    gate = np.zeros((D_MODEL, P), w.dtype)
    gate[:, 0:MH] = i_
    gate[:, 32:32 + MH] = f_
    out["win"] = _tiles(np.concatenate([gate, u_, q_, k_, v_, c_, h_, b_, o_], axis=1), KD, M_END)
    order = lambda a: np.concatenate([a[768:1024], a[512:768], a[0:512]])
    out["wout"] = _tiles(order(g("w_out")), KD, KD)
    prm = np.zeros((P, NPRM), np.float32)

    def put(n, a):
        prm[0:a.shape[0], slice(*PRM[n])] = a.reshape(a.shape[0], -1)

    put("norm_g", np.moveaxis(_features(g("norm_g")), 1, 2))
    put("mix_g", _features(order(g("mix_g"))))
    put("conv_w", np.moveaxis(_features(g("conv_w")), 1, 2))
    put("s5_d", _features(g("s5_d")))
    states = lambda a: np.moveaxis(a.reshape((SJ, P) + a.shape[2:]), 0, 1)
    put("a_re", states(g("s5_a_re")))
    put("a_im", states(g("s5_a_im")))
    put("log_dt", states(np.repeat(g("s5_log_dt")[:, None], S5_P, axis=1)))
    put("gate_b", np.stack([g("ig_bias"), g("fg_bias")], axis=1))
    put("m0", g("state_mlstm_m").T)
    put("h0", np.stack([states(np.moveaxis(g(n), 0, -1)) for n in ("state_s5_re", "state_s5_im")], axis=1))
    put("conv0", _features(g("state_conv")))
    put("n0", g("state_mlstm_n").transpose(2, 1, 0))
    for n in ("re", "im"):
        put(f"c_{n}", states(g(f"s5_c_{n}").transpose(0, 2, 1)))
        b = g(f"s5_b_{n}").transpose(0, 2, 1).reshape(2, 4, 2, S5_CH, S5_P)
        bd = np.zeros((2, 4, 2, S5_CH, 2, S5_P), b.dtype)
        for gg in range(2):
            bd[:, :, gg, :, gg] = b[:, :, gg]
        put(f"b_{n}", np.moveaxis(bd.reshape(2, P, P), 0, 1))
    put("w_glu", np.moveaxis(g("w_glu").reshape(2, P, 256), 0, 1))
    out["prm"] = prm
    out["cst"], out["cst2"] = _constants()
    out["cT"] = g("state_mlstm_C").transpose(3, 1, 0, 2)
    return {n: np.ascontiguousarray(a) for n, a in out.items()}


def kernel(**inputs):
    import concourse.bacc as bacc
    from concourse.bass_utils import run_bass_kernel_spmd as run

    arrays = _layout(inputs)
    nc = bacc.Bacc("TRN2", target_bir_lowering=False, num_devices=1)
    A = {n: nc.dram_tensor(n, a.shape, F32, kind="ExternalInput").ap() for n, a in arrays.items()}
    for n, shape in _OUTS.items():
        A[n] = nc.dram_tensor(n, shape, F32, kind="ExternalOutput").ap()
    build(nc, A)
    r = run(nc, [arrays], core_ids=[0]).results[0]
    o = {n: np.asarray(r[n]) for n in _OUTS}
    rows = lambda a: np.moveaxis(a, (0, 1), (-1, -2)).reshape(a.shape[2:] + (-1,))
    y = rows(o["o_yT"])
    state = lambda a: np.moveaxis(a, 1, 0).reshape((S5_G, S5_P) + a.shape[2:])
    return (
        y[None, :SEQ], y[SEQ:].reshape(DEC_BATCH, DEC_SEQ, D_MODEL),
        o["o_pC"][:, :, :P].transpose(1, 2, 0)[None, None], o["o_pC"][:, :, P].T[None, None],
        o["o_m"][:, 0][None, None], state(o["o_ps5"][:, 0])[None, None], state(o["o_ps5"][:, 1])[None, None],
        rows(o["o_pconv"])[None, None],
        o["o_sC"].transpose(2, 1, 3, 0)[None], o["o_sn"].transpose(2, 1, 0)[None], o["o_m"][:, DEC_SEQ::DEC_SEQ].T[None],
        np.moveaxis(state(o["o_ss5"][:, 0]), -1, 0)[None], np.moveaxis(state(o["o_ss5"][:, 1]), -1, 0)[None],
        rows(o["o_sconv"])[None],
    )
```

```python
from contextlib import ExitStack

import numpy as np

import concourse.bass as bass
from concourse import mybir

F32 = mybir.dt.float32
F32R = mybir.dt.float32r
I32 = mybir.dt.int32
ALU = mybir.AluOpType
ACT = mybir.ActivationFunctionType

P = 128
D_MODEL, SEQ, DEC_BATCH, DEC_SEQ = 1024, 512, 8, 4
MH, DH, S5_G, S5_P, S5_CH, D_CONV, CONV_W = 4, 128, 16, 64, 16, 256, 3
D_FF = 2816
EPS = 1e-6
TS = DEC_BATCH * DEC_SEQ
T = SEQ + TS
HALF = T // 2
KD = D_MODEL // P
FT = D_FF // P
PARTS = (8, 8, 6)
assert sum(PARTS) == FT
UNIT = KD * P
NT = SEQ // P
NTT = NT + 1
LAST = T - P
SJ = S5_G * S5_P // P
CH = SEQ // 2
WBLK = [sum(SEQ - P * i for i in range(j)) for j in range(NT + 1)]
WCOL = WBLK[NT] + P
BIG = 3.0e38
MAGIC = 12582912.0

M_GATE, M_U, M_Q, M_K, M_V, M_CG, M_HC, M_BG, M_O, M_END = 0, 1, 3, 7, 11, 15, 17, 19, 21, 25
FFN_UNITS = 2 * FT + KD * len(PARTS)
MIX_BASE = FFN_UNITS
OUT_BASE = MIX_BASE + M_END
FFN2_BASE = OUT_BASE + KD

PRM = {}
_at = 0
for _n, _w in (("norm_g", 6 * KD), ("mix_g", KD), ("conv_w", CONV_W * 2), ("s5_d", 2), ("a_re", SJ), ("a_im", SJ),
               ("log_dt", SJ), ("gate_b", 2), ("m0", DEC_BATCH), ("h0", 2 * SJ * DEC_BATCH), ("conv0", 2 * DEC_BATCH * 2),
               ("n0", MH * DEC_BATCH), ("c_re", SJ * S5_CH), ("c_im", SJ * S5_CH), ("b_re", 2 * P), ("b_im", 2 * P), ("w_glu", 4 * P)):
    PRM[_n] = (_at, _at + _w)
    _at += _w
NPRM = _at
CST = {}
_at = 0
for _n, _w in (("ident", P), ("ones", 1), ("tri", P), ("bmask", P), ("batch", DEC_BATCH)):
    CST[_n] = (_at, _at + _w)
    _at += _w
NCST = _at
NCST2 = MH * P + CH
PI_BELOW = 3.1415925
INV_2PI = 0.15915494309189535
C1, C2, C3 = 6.28125, 0.0019350051879882812, 3.0199159819e-07
LN2_HI, LN2_LO, LOG2E = 0.693359375, -2.12194440e-4, 1.4426950408889634


def build(nc, A):
    with ExitStack() as ctx:
        place = [(nc.sbuf_base + 31) // 32 * 32]

        def sb(name, shape, dt=F32, at=None):
            n = int(np.prod(shape[1:])) * 4
            if at is None:
                at = place[0]
                place[0] += (n + 31) // 32 * 32
            return nc.alloc_sbuf_tensor_at(name, shape, dt, offset=at)

        def sem(name):
            return ctx.enter_context(nc.semaphore(name))

        ps = ctx.enter_context(nc.psum_tensor("ps", [P, 8, 512], F32))
        psf = ps[:].rearrange("p b c -> p (b c)")
        x = sb("x", [P, KD, T])
        xh = sb("xh", [P, KD, T], F32R)
        xl = sb("xl", [P, KD, T], F32R)
        raw = [sb(f"raw{i}", [P, UNIT]) for i in range(2)]
        wh = [sb(f"wh{i}", [P, UNIT], F32R) for i in range(2)]
        wl = [sb(f"wl{i}", [P, UNIT], F32R) for i in range(2)]
        act_t = sb("act_t", [P, 2, T])
        dve_t = sb("dve_t", [P, 2, T])
        y_at = place[0]
        y = sb("y", [P, KD, T])
        er_at = place[0]
        er = sb("er", [P, SJ, CH])
        ei = sb("ei", [P, SJ, CH])
        prm = sb("prm", [P, NPRM])
        cst = sb("cst", [P, NCST])
        gpost = sb("gpost", [P, 3, KD])
        stat = sb("stat", [P, 64])
        s5p = sb("s5p", [P, 18, SJ])
        cbd = sb("cbd", [P, 4, SJ, 32])
        arena_at = place[0]
        used = [0]

        def mix(name, *dims, alias=None, dt=F32):
            n = (int(np.prod(dims)) + 7) // 8 * 8
            if alias is None:
                alias = used[0]
                used[0] += n
            return sb(name, [P, *dims], dt, at=arena_at + 4 * alias)

        hh = sb("hh", [P, max(PARTS), T], F32R, at=arena_at)
        hl = sb("hl", [P, max(PARTS), T], F32R, at=arena_at + 4 * max(PARTS) * T)
        hid_end = 2 * max(PARTS) * T
        rot = mix("rot", 4, SEQ)
        prod = mix("prod", 4, SEQ)
        hst = mix("hst", 2, SEQ)
        ut = mix("ut", 2, T)
        wgt = sb("wgt", [P, MH, WCOL], at=arena_at)
        used[0] = max(used[0], MH * WCOL)
        vbig = mix("vbig", DEC_BATCH, P)
        q = mix("q", MH, T)
        k = mix("k", MH, T)
        V_AT = used[0]
        v = mix("v", MH, T)
        cg_at = arena_at + 4 * used[0]
        cg = mix("cg", 2, T)
        zp = mix("zp", 2, SEQ + 2)
        zs = mix("zs", 2, DEC_BATCH, DEC_SEQ + 2)
        gl = mix("gl", 2, T)
        mbc_at = arena_at + 4 * used[0]
        mbc = mix("mbc", MH, T)
        hs_at = arena_at + 4 * used[0]
        hs = mix("hs", 2, SJ, TS)
        used[0] += 8
        sbc = mix("sbc", MH, TS)
        cols = mix("cols", 60)
        hlast = mix("hlast", 2, SJ)
        s5o = mix("s5o", 2, SJ)
        s5so = mix("s5so", 2, SJ, DEC_BATCH)
        nst = mix("nst", MH, DEC_BATCH)
        v_at = arena_at + 4 * V_AT
        place[0] = arena_at + 4 * max(used[0], hid_end)
        assert place[0] <= nc.sbuf_usable_end, (place[0], nc.sbuf_usable_end)
        ang = sb("ang", [P, 5, CH], at=arena_at + 4 * hid_end)
        angd = sb("angd", [P, SJ, CH], at=arena_at + 4 * (hid_end + 5 * CH))
        cst2 = sb("cst2", [P, NCST2], at=cg_at)
        sel, tpos = cst2[:, 0:MH * P], cst2[:, MH * P:]
        acc = sb("acc", [P, T], at=mbc_at)
        bcs = sb("bcs", [P, T], at=mbc_at + 4 * T)
        pst = sb("pst", [P, MH, P + 1], at=hs_at)
        msc = dve_t[:, 0]
        rows = sb("rows", [P, 8, T], at=y_at)
        kn = sb("kn", [P, MH, NT, P], at=y_at)
        sn = sb("sn", [P, 2, MH, P], at=y_at + 4 * 2048)
        vw = sb("vw", [P, 2, NT, P + 1], at=y_at + 4 * 3072)
        qs = sb("qs", [P, TS], at=y_at + 4 * 4104)
        prodn = sb("prodn", [P, P], at=y_at + 4 * 4136)
        wkm = sb("wkm", [P, MH, DEC_BATCH], at=y_at + 4 * 4264)
        vn = v[:, :, 0:SEQ].rearrange("p h (a d) -> p h a d", a=NT)
        bus = sb("bus", [P, 2, SJ, TS], at=v_at)
        xs5 = sb("xs5", [P, 2, SJ, TS], at=v_at + 4 * 512)
        tmp5 = sb("tmp5", [P, 4, SJ, TS], at=v_at + 4 * 1024)
        cs = sb("cs", [P, MH, DEC_BATCH, P], at=er_at)

        prm_ = {n: prm[:, a:b] for n, (a, b) in PRM.items()}
        cst_ = {n: cst[:, a:b] for n, (a, b) in CST.items()}
        ident, ones = cst_["ident"], cst_["ones"]
        norm_g = prm_["norm_g"].rearrange("p (n k) -> p n k", n=6)
        bbd = {"re": prm_["b_re"].rearrange("p (h s) -> p h s", h=2), "im": prm_["b_im"].rearrange("p (h s) -> p h s", h=2)}
        c_re = prm_["c_re"].rearrange("p (j c) -> p j c", j=SJ)
        c_im = prm_["c_im"].rearrange("p (j c) -> p j c", j=SJ)
        h0 = prm_["h0"].rearrange("p (r j b) -> p r j b", r=2, j=SJ)
        conv0 = prm_["conv0"].rearrange("p (c b w) -> p c b w", c=2, w=2)
        n0 = prm_["n0"].rearrange("p (h b) -> p h b", h=MH)
        m0 = prm_["m0"][0:MH, :]
        R_G, R_F, R_E, R_B, R_GM, R_M, R_KEEP, R_BND = range(8)
        S5_STEP = (11, 12, 13, 14, 16, 17, 18, 19)
        R_IN = 24
        LRE, DT, THETA, MAG, FF, FHI, FLO, IDEN, AR, AI, FRE, FIM, S0, S1, S2, S3, S4, S5 = range(18)

        def halves(t):
            return t.rearrange("p (a c) -> p a c", a=2)

        def pair(b):
            return ps[:, b:b + 2, 0:HALF]

        def row(r, a=0, b=T):
            return rows[0:MH, r, a:b]

        def cols_of(at, norms=1):
            return stat[:, at:at + 8 * norms].rearrange("p (n c) -> p n c", n=norms)[:, :, 0:NTT]

        def starts(ap):
            return ap[:, SEQ:T:DEC_SEQ]

        raw_full = [sem(f"raw_full{i}") for i in range(2)]
        hi_done = sem("hi_done")
        split_done = sem("split_done")
        unit_used = sem("unit_used")
        xf_ready = sem("xf_ready")
        xh_ready = sem("xh_ready")
        xl_ready = sem("xl_ready")
        a_ready = sem("a_ready")
        bc_evac = sem("bc_evac")
        silu_ready = sem("silu_ready")
        h_ready = sem("h_ready")
        h_hi = sem("h_hi")
        h_lo = sem("h_lo")
        y_evac = sem("y_evac")
        ysq_ready = sem("ysq_ready")
        ysq_used = sem("ysq_used")
        xsq_ready = sem("xsq_ready")
        xsq_used = sem("xsq_used")
        xacc_ready = sem("xacc_ready")
        x_new = sem("x_new")
        stat_done = sem("stat_done")
        var_ready = sem("var_ready")
        std_ready = sem("std_ready")
        rcol_ready = sem("rcol_ready")
        bc_done = sem("bc_done")
        gain_in = sem("gain_in")
        cst_in = sem("cst_in")
        prm_in = sem("prm_in")
        x_in = [sem(f"x_in{i}") for i in range(4)]
        cs_in = sem("cs_in")
        out_dma = sem("out_dma")
        m_out = sem("m_out")
        dve_chain = sem("dve_chain")
        pool_chain = sem("pool_chain")
        s5_par = sem("s5_par")
        ang_ready = sem("ang_ready")
        e_sin = sem("e_sin")
        e_ready = sem("e_ready")
        f_ready = sem("f_ready")
        t_evac = sem("t_evac")
        o_ready = sem("o_ready")
        ga = sem("ga")
        gv = sem("gv")
        masks_ready = sem("masks_ready")
        bu_s = sem("bu_s")
        bus_evac = sem("bus_evac")
        hs_ready = sem("hs_ready")
        mb_done = sem("mb_done")
        mb_evac = sem("mb_evac")
        bu_done = sem("bu_done")
        rot_ready = sem("rot_ready")
        xrot_ready = sem("xrot_ready")
        prod_ready = sem("prod_ready")
        hst_ready = sem("hst_ready")
        ys_done = sem("ys_done")
        yss_done = sem("yss_done")
        ys_evac = sem("ys_evac")
        gelu_ready = sem("gelu_ready")
        glu_done = sem("glu_done")
        glu_sig = sem("glu_sig")
        outb_ready = sem("outb_ready")
        conv_used = sem("conv_used")
        outc_ready = sem("outc_ready")
        nat_done = sem("nat_done")
        nat_evac = sem("nat_evac")
        d_ready = sem("d_ready")
        w_exp = sem("w_exp")
        w_ready = sem("w_ready")
        sc_done = sem("sc_done")
        p_ready = sem("p_ready")
        qs_ready = sem("qs_ready")
        inter_done = sem("inter_done")
        vw_ready = sem("vw_ready")
        cdec_ready = sem("cdec_ready")
        cps_done = sem("cps_done")
        cps_used = sem("cps_used")
        num_done = sem("num_done")
        hso_ready = sem("hso_ready")
        st_done = sem("st_done")
        st_evac = sem("st_evac")
        s5_out = sem("s5_out")

        block = ctx.enter_context(nc.Block())
        OUTS_N = [0]

        @block.sync
        def _(spe):
            def load(u, par, src, cols=UNIT):
                spe.wait_ge(split_done, u + 1)
                spe.dma_start(raw[par][:, 0:cols], src).then_inc(raw_full[par], 16)

            def ffn(f, u0):
                w13, w2 = A[f"w13_{f}"], A[f"w2_{f}"]
                k0 = 0
                for n in PARTS:
                    first = 1 if f == 0 and k0 == 0 else 0
                    with spe.Fori(first, n) as i:
                        for c in range(2):
                            load(u0 + 2 * i + c, (u0 + c) % 2, w13[2 * k0 + 2 * i + c])
                    u0 += 2 * n
                    with spe.Fori(0, KD // 2) as i:
                        for c in range(2):
                            load(u0 + 2 * i + c, (u0 + c) % 2, w2[2 * i + c, :, k0 * P:(k0 + n) * P], n * P)
                    u0 += KD
                    k0 += n

            def store(dst, src):
                spe.dma_start(dst, src).then_inc(out_dma, 16)
                OUTS_N[0] += 1

            gains = slice(0, PRM["norm_g"][1])
            spe.dma_start(prm[:, gains], A["prm"][:, gains]).then_inc(gain_in, 16)
            spe.dma_start(x[:, 0:2], A["xT"][:, 0:2]).then_inc(x_in[0], 16)
            load(0, 0, A["w13_0"][0])
            for i in range(1, 4):
                spe.dma_start(x[:, 2 * i:2 * i + 2], A["xT"][:, 2 * i:2 * i + 2]).then_inc(x_in[i], 16)
                if i == 1:
                    spe.dma_start(cst[:], A["cst"]).then_inc(cst_in, 16)
            load(1, 1, A["w13_0"][1])
            spe.dma_start(prm[:, gains.stop:], A["prm"][:, gains.stop:]).then_inc(prm_in, 16)
            spe.dma_start(cst2[:], A["cst2"]).then_inc(prm_in, 16)
            ffn(0, 0)
            for i in range(M_END):
                u = MIX_BASE + i
                load(u, u % 2, A["win"][i])
                if i == 9:
                    spe.wait_ge(gv, 14)
                    spe.dma_start(A["o_m"], row(R_E, SEQ - 1, T)).then_inc(m_out, 16)
                if i == 22:
                    spe.wait_ge(hst_ready, SJ)
                    spe.wait_ge(prod_ready, SJ)
                    spe.dma_start(cs[:], A["cT"]).then_inc(cs_in, 16)
                    spe.wait_ge(s5_out, 1)
                    store(A["o_ps5"], s5o[:])
                    store(A["o_ss5"], s5so[:])
                if i == 24:
                    spe.wait_ge(outc_ready, 2)
                    store(A["o_pconv"], zp[:, :, SEQ:SEQ + 2])
                    store(A["o_sconv"], zs[:, :, :, DEC_SEQ:DEC_SEQ + 2])
            load(OUT_BASE, OUT_BASE % 2, A["wout"][0])
            load(OUT_BASE + 1, (OUT_BASE + 1) % 2, A["wout"][1])
            for h in range(MH):
                spe.wait_ge(cps_used, 2 * h + 2)
                store(A["o_sC"][:, h], cs[:, h])
            spe.wait_ge(st_evac, MH)
            store(A["o_pC"], pst[:])
            store(A["o_sn"], nst[:])
            for m in range(2, KD):
                load(OUT_BASE + m, (OUT_BASE + m) % 2, A["wout"][m])
            ffn(1, FFN2_BASE)
            for kk in range(KD):
                spe.wait_ge(x_new, 2 * KD + kk + 1)
                store(A["o_yT"][:, kk], x[:, kk])
            spe.wait_ge(m_out, 16)
            spe.wait_ge(out_dma, 16 * OUTS_N[0])

        @block.scalar
        def _(act):
            cnt = {"norm": 0, "xs": 0, "xf": 0, "bc": 0, "e": 0, "sq": 0}

            def split(u, par, half, cols=UNIT):
                act.wait_ge(raw_full[par], 16 * (half + 1))
                act.wait_ge(unit_used, u + 1)
                nc.scalar.copy(wh[par][:, 0:cols], raw[par][:, 0:cols]).then_inc(hi_done, 1)

            def silu(hm, s):
                act.wait_ge(a_ready, hm + 1)
                nc.scalar.activation(act_t[:, s], act_t[:, s], ACT.Silu).then_inc(silu_ready, 1)

            def hidden_hi(hm, s, mi):
                act.wait_ge(h_ready, hm + 3)
                nc.scalar.copy(hh[:, mi, :], dve_t[:, s]).then_inc(h_hi, 1)

            def down_evac(m, s, yb, qb, last):
                if last:
                    act.wait_ge(y_evac, yb + m + 3)
                    act.wait_ge(ysq_used, qb + m + 1)
                    nc.scalar.activation(act_t[:, s], y[:, m, :], ACT.Square).then_inc(ysq_ready, 1)

            def angles(n):
                for _ in range(n):
                    j = cnt["e"]
                    cnt["e"] += 1
                    act.wait_ge(ang_ready, j + 1)
                    nc.scalar.activation(ei[:, j], angd[:, j], ACT.Sin, scale=2 * PI_BELOW).then_inc(e_sin, 1)
                    nc.scalar.activation(er[:, j], angd[:, j], ACT.Sin, scale=PI_BELOW).then_inc(e_sin, 1)
                    act.wait_ge(e_sin, 3 * j + 2)
                    nc.scalar.activation(er[:, j], er[:, j], ACT.Square).then_inc(e_sin, 1)

            def ffn(f, u0, hb, yb, qb, before, inputs):
                prev = before
                for p, n in enumerate(PARTS):
                    last = p == len(PARTS) - 1
                    half = lambda c: (u0 + c) // 2
                    split(u0, u0 % 2, half(0))
                    prev[0]()
                    if p:
                        split(u0 + 1, (u0 + 1) % 2, half(1))
                        prev[1]()
                    elif f == 0:
                        inputs()
                        split(u0 + 1, (u0 + 1) % 2, half(1))
                    else:
                        prev[1]()
                        split(u0 + 1, (u0 + 1) % 2, half(1))
                        inputs()
                    split(u0 + 2, u0 % 2, half(2))
                    if p:
                        silu(hb, 0)
                        split(u0 + 3, (u0 + 1) % 2, half(3))
                    else:
                        root()
                        split(u0 + 3, (u0 + 1) % 2, half(3))
                        scales_out(bcs[:])
                        silu(hb, 0)
                    hidden_hi(hb, 0, 0)
                    with act.Fori(1, n // 2) as i:
                        for c in range(4):
                            split(u0 + 4 * i + c, (u0 + c) % 2, (u0 + c) // 2 + 2 * i)
                            mi, s = 2 * i - 1 + c // 2, (c // 2 + 1) % 2
                            if c % 2:
                                hidden_hi(hb + mi, s, mi)
                            else:
                                silu(hb + mi, s)
                    u1 = u0 + 2 * n
                    if f == 0 and p:
                        angles(4)
                    split(u1, u1 % 2, u1 // 2, n * P)
                    silu(hb + n - 1, 1)
                    split(u1 + 1, (u1 + 1) % 2, (u1 + 1) // 2, n * P)
                    hidden_hi(hb + n - 1, 1, n - 1)
                    if last:
                        sqrt_table()
                    with act.Fori(1, KD // 2) as i:
                        for c in range(2):
                            split(u1 + 2 * i + c, (u1 + c) % 2, (u1 + c) // 2 + i, n * P)
                            down_evac(2 * i - 2 + c, c, yb, qb, last)
                    prev = [lambda yb=yb, last=last: down_evac(6, 0, yb, qb, last),
                            lambda yb=yb, last=last: down_evac(7, 1, yb, qb, last)]
                    u0 = u1 + KD
                    hb += n
                    yb += KD
                return prev

            def sqrt_table():
                nc.scalar.activation(stat[0:1, 62:63], stat[0:1, 62:63], ACT.Sqrt)

            def root(norms=1):
                n = cnt["norm"]
                cnt["norm"] += 1
                act.wait_ge(var_ready, n + 1)
                nc.scalar.activation(cols_of(16, norms), cols_of(0, norms), ACT.Sqrt).then_inc(std_ready, 1)

            def square(src, wait):
                n = cnt["sq"]
                cnt["sq"] += 1
                wait()
                if n >= 2:
                    act.wait_ge(xsq_used, n - 1)
                nc.scalar.activation(act_t[:, n % 2], src, ACT.Square).then_inc(xsq_ready, 1)

            def hi_part(kk):
                e = cnt["xs"]
                cnt["xs"] += 1
                cnt["xf"] += 1
                act.wait_ge(xf_ready, cnt["xf"])
                nc.scalar.copy(xh[:, kk], dve_t[:, e % 2]).then_inc(xh_ready, 1)

            def inputs(g, ready):
                for kk in range(KD):
                    ready(kk)
                    nc.scalar.activation(xh[:, kk], x[:, kk], ACT.Copy, scale=norm_g[:, g, kk:kk + 1]).then_inc(xh_ready, 1)
                    cnt["xs"] += 1
                    square(x[:, kk], lambda: None)

            def scales_out(dst):
                cnt["bc"] += 1
                act.wait_ge(bc_done, cnt["norm"])
                nc.scalar.copy(dst, psf[:, 6 * 512:6 * 512 + T]).then_inc(bc_evac, 1)

            def x_loaded(kk):
                if kk == 0:
                    act.wait_ge(gain_in, 16)
                    act.wait_ge(split_done, 2)
                    sqrt_table()
                act.wait_ge(x_in[kk // 2], 16)

            nothing = lambda: None
            tail = ffn(0, 0, 0, 0, 0, [nothing, nothing], lambda: inputs(0, x_loaded))

            def mix_split(i):
                u = MIX_BASE + i
                split(u, u % 2, u // 2)

            mix_split(0)
            tail[0]()
            tail[1]()
            mix_split(1)
            root()
            inputs(2, lambda kk: act.wait_ge(x_new, kk + 1))

            def gates(s):
                if s == 4:
                    act.wait_ge(gv, 2)
                    nc.scalar.activation(row(R_E), row(R_F), ACT.Abs).then_inc(ga, 1)
                    act.wait_ge(ga, 1)
                    nc.scalar.activation(row(R_E), row(R_E), ACT.Exp, scale=-1.0).then_inc(ga, 1)
                if s == 5:
                    act.wait_ge(gv, 3)
                    nc.scalar.activation(row(R_E), row(R_E), ACT.Ln).then_inc(ga, 1)
                if s == 6:
                    act.wait_ge(gv, 14)
                    nc.scalar.activation(row(R_GM), row(R_GM), ACT.Exp).then_inc(ga, 1)
                    nc.scalar.activation(row(R_B), row(R_E), ACT.Exp, scale=-1.0).then_inc(ga, 1)
                    nc.scalar.activation(row(R_F, SEQ), row(R_F, SEQ), ACT.Exp).then_inc(ga, 1)

            def weights(h):
                act.wait_ge(d_ready, h + 1)
                nc.scalar.activation(wgt[:, h, 0:WBLK[NT]], wgt[:, h, 0:WBLK[NT]], ACT.Exp, scale=-1.0).then_inc(w_exp, 1)
                nc.scalar.activation(wgt[0:TS, h, WBLK[NT]:], wgt[0:TS, h, WBLK[NT]:], ACT.Exp, scale=-1.0).then_inc(w_exp, 1)

            def natural(h):
                if h == 0:
                    act.wait_ge(m_out, 16)
                act.wait_ge(nat_done, h + 1)
                nc.scalar.copy(kn[:, h], ps[:, 4, :].rearrange("p (a d) -> p a d", a=NT)).then_inc(nat_evac, 1)
                nc.scalar.copy(vn[:, h], ps[:, 5, :].rearrange("p (a d) -> p a d", a=NT)).then_inc(nat_evac, 1)

            for s in range(2, M_END + 2):
                if s < M_END:
                    mix_split(s)
                else:
                    u = OUT_BASE + s - M_END
                    split(u, u % 2, u // 2)
                if s == 2:
                    root()
                    scales_out(msc)
                gates(s)
                if s - 2 >= M_O:
                    act.wait_ge(t_evac, s - 1)
                    o_h = mbc[:, s - 2 - M_O]
                    nc.scalar.activation(o_h, o_h, ACT.Sigmoid).then_inc(o_ready, 1)
                if s == 6:
                    act.wait_ge(bu_s, 1)
                    for g in range(4):
                        nc.scalar.copy(bus[:, :, g::4], ps[:, 4 + g, 0:4 * TS].rearrange("p (r j t) -> p r j t", r=2, t=TS))\
                            .then_inc(bus_evac, 1)
                if s == 8:
                    act.wait_ge(mb_done, 1)
                    nc.scalar.copy(mbc[:, :, 0:SEQ], ps[:, 4:8, :]).then_inc(mb_evac, 1)
                if s == 9:
                    act.wait_ge(mb_done, 2)
                    sv = ps[:, 4, 0:2 * MH * TS].rearrange("p (r h t) -> p r h t", r=2, h=MH)
                    nc.scalar.copy(mbc[:, :, SEQ:T], sv[:, 0]).then_inc(mb_evac, 1)
                    nc.scalar.copy(sbc[:], sv[:, 1]).then_inc(mb_evac, 1)
                    nc.scalar.copy(cols[:, 0:52], ps[:, 5, 0:52]).then_inc(mb_evac, 1)
                    nc.scalar.copy(cols[0:TS, 52:60], ps[0:TS, 5, 52:60]).then_inc(mb_evac, 1)
                if s == 22:
                    weights(0)
                    weights(1)
                if s == 23:
                    act.wait_ge(ys_evac, 1)
                    nc.scalar.activation(gl[:], gl[:], ACT.Gelu_apprx_tanh).then_inc(gelu_ready, 1)
                    weights(2)
                    weights(3)
                if s >= 23:
                    natural(s - 23)
            for m in range(2):
                act.wait_ge(glu_done, m + 1)
                act.wait_ge(conv_used, 4)
                nc.scalar.activation(halves(act_t[:, m]), pair(6 if m == 0 else 4), ACT.Sigmoid).then_inc(glu_sig, 1)
            act.wait_ge(nat_done, MH + 1)
            nc.scalar.copy(sn[0:TS, 0], ps[0:TS, 6, :].rearrange("p (h d) -> p h d", h=MH)).then_inc(nat_evac, 1)
            nc.scalar.copy(sn[0:TS, 1], ps[0:TS, 7, :].rearrange("p (h d) -> p h d", h=MH)).then_inc(nat_evac, 1)
            act.wait_ge(outb_ready, 2)
            act.wait_ge(outc_ready, 2)
            for n, t in enumerate((cg, gl)):
                for c in range(2):
                    square(t[:, c], lambda: None)
            root(2)
            for kk in range(4):
                hi_part(kk)
            for h in range(MH + 1):
                if h >= 1:
                    root()
                    hi_part(3 + h)
                if h < MH:
                    square(mbc[:, h], lambda: act.wait_ge(hso_ready, h + 1))

            def out_sq(m):
                act.wait_ge(y_evac, 24 + m + 3)
                act.wait_ge(ysq_used, KD + m + 1)
                act.wait_ge(xsq_used, cnt["sq"])
                nc.scalar.activation(act_t[:, m % 2], y[:, m], ACT.Square).then_inc(ysq_ready, 1)

            for m in range(2, KD):
                u = OUT_BASE + m
                split(u, u % 2, u // 2)
                out_sq(m - 2)

            def ffn2_inputs():
                root()
                inputs(4, lambda kk: act.wait_ge(x_new, KD + kk + 1))

            tail = ffn(1, FFN2_BASE, FT, 32, 2 * KD, [lambda: out_sq(6), lambda: out_sq(7)], ffn2_inputs)
            tail[0]()
            tail[1]()
            root()

        @block.vector
        def _(dve):
            V = nc.vector
            chain = [0]

            def link(ins):
                chain[0] += 1
                ins.then_inc(dve_chain, 1)
                dve.wait_ge(dve_chain, chain[0])

            def note(ins):
                chain[0] += 1
                ins.then_inc(dve_chain, 1)

            def settle():
                dve.wait_ge(dve_chain, chain[0])

            cnt = {"norm": 0, "xs": 0, "bc": 0}

            def lo_part(u, par, cols=UNIT):
                dve.wait_ge(hi_done, u + 1)
                V.tensor_tensor(wl[par][:, 0:cols], raw[par][:, 0:cols], wh[par][:, 0:cols].bitcast(F32),
                                ALU.subtract).then_inc(split_done, 1)

            def up_first(hm, s, u):
                dve.wait_ge(unit_used, u + 3)
                dve.wait_ge(h_ready, hm + 1)
                V.tensor_tensor(halves(act_t[:, s]), pair(4 * s), halves(bcs[:]), ALU.mult).then_inc(a_ready, 1)

            def up_second(hm, s, u, mi):
                dve.wait_ge(silu_ready, hm + 1)
                dve.wait_ge(unit_used, u + 3)
                V.tensor_tensor(halves(dve_t[:, s]), pair(4 * s + 2), halves(act_t[:, s]), ALU.mult).then_inc(h_ready, 1)
                dve.wait_ge(h_hi, hm + 1)
                V.tensor_tensor(hl[:, mi, :], dve_t[:, s], hh[:, mi, :].bitcast(F32), ALU.subtract).then_inc(h_lo, 1)

            def down_evac(m, s, yb, qb, u, p, last, banks):
                dve.wait_ge(unit_used, u + 3)
                if p == 0:
                    V.tensor_copy(halves(y[:, m, :]), pair(banks)).then_inc(y_evac, 1)
                else:
                    dve.wait_ge(y_evac, yb + m - KD + 3)
                    V.tensor_tensor(halves(y[:, m, :]), pair(banks), halves(y[:, m, :]), ALU.add).then_inc(y_evac, 1)
                if last:
                    dve.wait_ge(ysq_ready, qb + m + 1)
                    dve.wait_ge(ysq_used, qb + m + 2)
                    V.tensor_tensor(acc[:], acc[:], act_t[:, s], ALU.add).then_inc(ysq_used, 1)

            def ffn(f, u0, hb, yb, qb, before, inputs, between=lambda p, n: None):
                prev = before
                for p, n in enumerate(PARTS):
                    last = p == len(PARTS) - 1
                    lo_part(u0, u0 % 2)
                    prev[0]()
                    if p:
                        lo_part(u0 + 1, (u0 + 1) % 2)
                        prev[1]()
                    elif u0 == 0:
                        inputs()
                        lo_part(u0 + 1, (u0 + 1) % 2)
                    else:
                        prev[1]()
                        lo_part(u0 + 1, (u0 + 1) % 2)
                        inputs()
                    lo_part(u0 + 2, u0 % 2)
                    if p:
                        up_first(hb, 0, u0)
                        lo_part(u0 + 3, (u0 + 1) % 2)
                    else:
                        token_scale(7, D_MODEL, R_IN)
                        lo_part(u0 + 3, (u0 + 1) % 2)
                        cnt["bc"] += 1
                        dve.wait_ge(bc_evac, cnt["bc"])
                        up_first(hb, 0, u0)
                    up_second(hb, 0, u0 + 1, 0)
                    between(p, 0)
                    with dve.Fori(1, n // 2) as i:
                        for c in range(4):
                            lo_part(u0 + 4 * i + c, (u0 + c) % 2)
                            mi, s = 2 * i - 1 + c // 2, (c // 2 + 1) % 2
                            if c % 2:
                                up_second(hb + mi, s, u0 + 2 * mi + 1, mi)
                            else:
                                up_first(hb + mi, s, u0 + 2 * mi)
                    u1 = u0 + 2 * n
                    lo_part(u1, u1 % 2, n * P)
                    up_first(hb + n - 1, 1, u1 - 2)
                    between(p, 1)
                    lo_part(u1 + 1, (u1 + 1) % 2, n * P)
                    up_second(hb + n - 1, 1, u1 - 1, n - 1)
                    between(p, 2)
                    with dve.Fori(1, KD // 2) as i:
                        for c in range(2):
                            lo_part(u1 + 2 * i + c, (u1 + c) % 2, n * P)
                            m = 2 * i - 2 + c
                            down_evac(m, c, yb, qb, u1 + m, p, last, 2 * c)
                    prev = [lambda yb=yb, p=p, last=last, u1=u1: down_evac(6, 0, yb, qb, u1 + 6, p, last, 0),
                            lambda yb=yb, p=p, last=last, u1=u1: down_evac(7, 1, yb, qb, u1 + 7, p, last, 2)]
                    u0 = u1 + KD
                    hb += n
                    yb += KD
                return prev

            def scale_col(bank, width, norms=1):
                n = cnt["norm"]
                cnt["norm"] += 1
                dve.wait_ge(stat_done, n + 1)
                sums = ps[:, bank, 0:8 * norms].rearrange("p (n c) -> p n c", n=norms)[:, :, 0:NTT]
                V.tensor_scalar(cols_of(0, norms), sums, 1.0 / width, EPS, ALU.mult, ALU.add).then_inc(var_ready, 1)
                dve.wait_ge(std_ready, n + 1)
                V.reciprocal(cols_of(16, norms), cols_of(16, norms)).then_inc(rcol_ready, 1)
                dve.wait_ge(bc_done, n + 1)

            def lo_of(kk, e):
                dve.wait_ge(xh_ready, e + 1)
                V.tensor_tensor(xl[:, kk], dve_t[:, e % 2], xh[:, kk].bitcast(F32), ALU.subtract).then_inc(xl_ready, 1)

            def scaled(tiles):
                last = None
                for kk, write in tiles:
                    e = cnt["xs"]
                    cnt["xs"] += 1
                    if e >= 2:
                        dve.wait_ge(xh_ready, e - 1)
                        dve.wait_ge(xl_ready, e - 1)
                    write(dve_t[:, e % 2])
                    if last:
                        lo_of(*last)
                    last = (kk, e)
                lo_of(*last)

            def input_lo(g, kk):
                dve.wait_ge(xh_ready, cnt["xs"] + 1)
                V.scalar_tensor_tensor(xl[:, kk], x[:, kk], norm_g[:, g, kk:kk + 1], xh[:, kk].bitcast(F32), ALU.mult,
                                       ALU.subtract).then_inc(xl_ready, 1)
                cnt["xs"] += 1

            def token_scale(bank, width, at):
                n = cnt["norm"]
                cnt["norm"] += 1
                dve.wait_ge(stat_done, n + 1)
                V.tensor_scalar(stat[:, 0:NTT], ps[:, bank, 0:NTT], 1.0 / width, EPS, ALU.mult, ALU.add).then_inc(var_ready, 1)
                dve.wait_ge(std_ready, n + 1)
                r_in = stat[:, at:at + NTT]
                V.reciprocal(r_in, stat[:, 16:16 + NTT]).then_inc(rcol_ready, 1)
                dve.wait_ge(rcol_ready, n + 1)
                link(V.scalar_tensor_tensor(stat[:, at + 8:at + 8 + NTT], r_in, 1.0 / D_MODEL, r_in, ALU.mult, ALU.mult))
                link(V.memset(acc[:], 0.0))

            def ffn_scale(bank):
                n = cnt["norm"]
                cnt["norm"] += 1
                dve.wait_ge(stat_done, n + 1)
                link(V.tensor_tensor(stat[:, 0:NTT], ps[:, bank, 0:NTT], stat[:, R_IN + 8:R_IN + 8 + NTT], ALU.mult))
                V.tensor_scalar(stat[:, 0:NTT], stat[:, 0:NTT], 1.0, EPS, ALU.mult, ALU.add).then_inc(var_ready, 1)
                dve.wait_ge(std_ready, n + 1)
                link(V.reciprocal(stat[:, 16:16 + NTT], stat[:, 16:16 + NTT]))
                V.tensor_tensor(stat[:, 16:16 + NTT], stat[:, 16:16 + NTT], stat[:, R_IN:R_IN + NTT], ALU.mult)\
                    .then_inc(rcol_ready, 1)
                dve.wait_ge(bc_done, n + 1)

            def post_norm(g, scale, after_x=lambda kk: None):
                scale()
                bc = psf[:, 4 * 512:4 * 512 + T]
                for kk in range(KD + 1):
                    if kk < KD:
                        note(V.tensor_tensor(y[:, kk], y[:, kk], bc, ALU.mult))
                        done = chain[0]
                    if kk:
                        dve.wait_ge(dve_chain, before)
                        V.scalar_tensor_tensor(x[:, kk - 1], y[:, kk - 1], gpost[:, g, kk - 1:kk], x[:, kk - 1],
                                               ALU.mult, ALU.add).then_inc(x_new, 1)
                    if kk > 1:
                        after_x(kk - 2)
                    before = done
                after_x(KD - 1)

            V.memset(stat[:, 62:64], 0.0).then_inc(split_done, 2)
            V.memset(stat[:, 57:58], 0.0).then_inc(unit_used, 2)
            V.memset(stat[:, 58:59], 0.0).then_inc(h_ready, 2)
            V.memset(stat[:, 59:60], 0.0).then_inc(y_evac, 2)
            V.memset(stat[:, 60:61], 0.0).then_inc(ysq_used, 2)
            note(V.memset(cbd[:], 0.0))

            def par(r):
                return s5p[:, r, :]

            def exp_to(out, src):
                link(V.tensor_scalar(par(S0), src, LOG2E, MAGIC, ALU.mult, ALU.add))
                link(V.tensor_scalar(par(S0), par(S0), -MAGIC, None, ALU.add))
                link(V.tensor_scalar(par(S0), par(S0), -126.0, 127.0, ALU.max, ALU.min))
                link(V.scalar_tensor_tensor(par(S1), par(S0), -LN2_HI, src, ALU.mult, ALU.add))
                link(V.scalar_tensor_tensor(par(S1), par(S0), -LN2_LO, par(S1), ALU.mult, ALU.add))
                link(V.tensor_scalar(par(S2), par(S1), 1.0 / 5040, None, ALU.mult))
                for c in (720, 120, 24, 6, 2, 1):
                    link(V.scalar_tensor_tensor(par(S2), par(S2), 1.0 / c, par(S1), ALU.add, ALU.mult))
                link(V.tensor_scalar(par(S3).bitcast(I32), par(S0), 127.0, 8388608.0, ALU.add, ALU.mult))
                link(V.scalar_tensor_tensor(out, par(S2), 1.0, par(S3), ALU.add, ALU.mult))

            def reduce(out, src, parts):
                link(V.scalar_tensor_tensor(out, par(S0), -parts[0], src, ALU.mult, ALU.add))
                for c in parts[1:]:
                    link(V.scalar_tensor_tensor(out, par(S0), -c, out, ALU.mult, ALU.add))

            a_im = prm_["a_im"]

            def s5_scalars(p, n):
                if p == 0 and n == 0:
                    dve.wait_ge(prm_in, 32)
                    settle()
                    note(V.tensor_scalar(gpost[:, 0], norm_g[:, 1], 0.5, None, ALU.mult))
                    note(V.tensor_scalar(gpost[:, 1], norm_g[:, 3], 1.0, None, ALU.mult))
                    note(V.tensor_scalar(gpost[:, 2], norm_g[:, 5], 0.5, None, ALU.mult))
                    link(V.tensor_scalar(par(LRE), prm_["a_re"], -1e-4, None, ALU.min))
                    exp_to(par(DT), prm_["log_dt"])
                elif p == 0 and n == 1:
                    link(V.tensor_tensor(par(THETA), a_im, par(DT), ALU.mult))
                    link(V.tensor_tensor(par(S4), par(LRE), par(DT), ALU.mult))
                    exp_to(par(MAG), par(S4))
                elif p == 0 and n == 2:
                    link(V.tensor_scalar(par(S0), par(THETA), INV_2PI, MAGIC, ALU.mult, ALU.add))
                    link(V.tensor_scalar(par(S0), par(S0), -MAGIC, None, ALU.add))
                    reduce(par(S4), par(THETA), (C1, C2, C3))
                    link(V.tensor_scalar(par(FF), par(S4), INV_2PI, None, ALU.mult))
                    link(V.tensor_scalar(par(S0), par(FF), 4096.0, MAGIC, ALU.mult, ALU.add))
                    link(V.tensor_scalar(par(FHI), par(S0), -MAGIC, 1.0 / 4096, ALU.add, ALU.mult))
                    link(V.tensor_copy(par(S0), par(FHI)))
                    reduce(par(S5), par(S4), (C1, C2, C3))
                    link(V.tensor_scalar(par(FLO), par(S5), INV_2PI, None, ALU.mult))
                elif p == 1 and n == 0:
                    link(V.tensor_tensor(par(S0), par(LRE), par(LRE), ALU.mult))
                    link(V.tensor_tensor(par(S1), a_im, a_im, ALU.mult))
                    link(V.tensor_tensor(par(S0), par(S0), par(S1), ALU.add))
                    V.reciprocal(par(IDEN), par(S0)).then_inc(s5_par, 1)

            def x_loaded(kk):
                if kk == 0:
                    dve.wait_ge(gain_in, 16)
                dve.wait_ge(x_in[kk // 2], 16)

            def ffn1_inputs():
                for kk in range(KD):
                    x_loaded(kk)
                    input_lo(0, kk)

            nothing = lambda: None
            tail = ffn(0, 0, 0, 0, 0, [nothing, nothing], ffn1_inputs, s5_scalars)
            lo_part(MIX_BASE, MIX_BASE % 2)
            tail[0]()
            tail[1]()
            lo_part(MIX_BASE + 1, (MIX_BASE + 1) % 2)
            post_norm(0, lambda: ffn_scale(6), lambda kk: input_lo(2, kk))

            def gate(s):
                def step(ins):
                    gate.n += 1
                    ins.then_inc(gv, 1)
                    dve.wait_ge(gv, gate.n)
                if s == 3:
                    step(V.tensor_scalar(row(R_G), row(R_G), prm_["gate_b"][0:MH, 0:1], None, ALU.add))
                    step(V.tensor_scalar(row(R_F), row(R_F), prm_["gate_b"][0:MH, 1:2], None, ALU.add))
                if s == 4:
                    dve.wait_ge(ga, 2)
                    step(V.tensor_scalar(row(R_E), row(R_E), 1.0, None, ALU.add))
                if s == 5:
                    dve.wait_ge(ga, 3)
                    dve.wait_ge(masks_ready, 4)
                    step(V.scalar_tensor_tensor(row(R_F), row(R_F), 0.0, row(R_E), ALU.min, ALU.subtract))
                    step(V.tensor_tensor_scan(row(R_B), row(R_KEEP), row(R_F), 0.0, ALU.mult, ALU.add))
                    step(V.tensor_tensor(row(R_G), row(R_G), row(R_B), ALU.subtract))
                    step(V.tensor_copy(row(R_GM), row(R_G)))
                    step(V.tensor_scalar(row(R_GM, 0, 1), row(R_GM, 0, 1), 0.0, None, ALU.max))
                    step(V.tensor_tensor(starts(row(R_GM)), starts(row(R_GM)), m0, ALU.max))
                    step(V.tensor_tensor_scan(row(R_M), row(R_BND), row(R_GM), 0.0, ALU.min, ALU.max))
                    step(V.tensor_scalar(row(R_GM, 0, SEQ), row(R_G, 0, SEQ), row(R_M, SEQ - 1, SEQ), None, ALU.subtract))
                    bt = lambda r: row(r, SEQ).rearrange("p (b t) -> p b t", b=DEC_BATCH)
                    step(V.tensor_tensor(bt(R_GM), bt(R_G), bt(R_M)[:, :, DEC_SEQ - 1:].to_broadcast([MH, DEC_BATCH, DEC_SEQ]),
                                         ALU.subtract))
                    step(V.tensor_tensor(row(R_E), row(R_B), row(R_M), ALU.add))
                    step(V.tensor_tensor(bt(R_F), m0.unsqueeze(2).to_broadcast([MH, DEC_BATCH, DEC_SEQ]), bt(R_M), ALU.subtract))
            gate.n = 0

            def evac(i):
                dve.wait_ge(unit_used, MIX_BASE + i + 3)

                def take(dst, factor=1.0):
                    b = 4 if i == 2 else 2 * (i % 2)
                    V.scalar_tensor_tensor(halves(dst), pair(b), factor, halves(msc), ALU.mult, ALU.mult).then_inc(t_evac, 1)

                if i == M_GATE:
                    dve.wait_ge(bc_evac, cnt["bc"])
                    for a, r in ((0, R_G), (32, R_F)):
                        link(V.tensor_tensor(halves(row(r)), ps[a:a + MH, 0:2, 0:HALF], halves(msc[a:a + MH]), ALU.mult))
                    V.memset(stat[:, 53:54], 0.0).then_inc(t_evac, 1)
                elif i < M_Q:
                    take(ut[:, i - M_U])
                elif i < M_K:
                    take(q[:, i - M_Q])
                elif i < M_V:
                    take(k[:, i - M_K], DH ** -0.5)
                elif i < M_CG:
                    if i == M_V:
                        dve.wait_ge(hs_ready, 1)
                    take(v[:, i - M_V])
                elif i < M_HC:
                    if i == M_CG:
                        dve.wait_ge(mb_evac, 5)
                    take(cg[:, i - M_CG])
                elif i < M_O:
                    take(act_t[:, (i - M_HC) % 2])
                else:
                    take(mbc[:, i - M_O])
                dve.wait_ge(t_evac, i + 1)

            def s5_in(j):
                dve.wait_ge(bu_done, j + 1)
                e_re = er[:, j].unsqueeze(1).to_broadcast([P, 2, CH])
                e_im = ei[:, j].unsqueeze(1).to_broadcast([P, 2, CH])
                if j == 0:
                    dve.wait_ge(f_ready, 1)
                else:
                    dve.wait_ge(xrot_ready, 2 * j)
                two = lambda t: t.rearrange("p (a c) -> p a c", a=2)
                xr, xi = two(ps[:, 4, :]), two(ps[:, 5, :])
                for n, (a, b) in enumerate(((xr, e_re), (xi, e_im), (xi, e_re), (xr, e_im))):
                    V.tensor_tensor(two(rot[:, n]), a, b, ALU.mult).then_inc(rot_ready, 1)

            def s5_scan(j):
                mag = s5p[:, MAG, j:j + 1].to_broadcast([P, CH])
                e_r, e_i = er[:, j, CH - 1:CH], ei[:, j, CH - 1:CH]
                dve.wait_ge(xrot_ready, 2 * j + 2)
                gr, gi = rot[:, 0], rot[:, 2]
                note(V.tensor_tensor_scan(gr[:, 0:CH], mag, gr[:, 0:CH], 0.0, ALU.mult, ALU.add))
                note(V.tensor_tensor_scan(gi[:, 0:CH], mag, gi[:, 0:CH], 0.0, ALU.mult, ALU.add))
                settle()
                last_r, last_i = gr[:, CH - 1:CH], gi[:, CH - 1:CH]
                note(V.tensor_tensor(stat[:, 48:49], last_i, e_i, ALU.mult))
                note(V.tensor_tensor(stat[:, 49:50], last_r, e_i, ALU.mult))
                settle()
                note(V.scalar_tensor_tensor(stat[:, 50:51], last_r, e_r, stat[:, 48:49], ALU.mult, ALU.subtract))
                note(V.scalar_tensor_tensor(stat[:, 51:52], last_i, e_r, stat[:, 49:50], ALU.mult, ALU.add))
                settle()
                note(V.tensor_tensor_scan(gr[:, CH:], mag, gr[:, CH:], stat[:, 50:51], ALU.mult, ALU.add))
                note(V.tensor_tensor_scan(gi[:, CH:], mag, gi[:, CH:], stat[:, 51:52], ALU.mult, ALU.add))
                settle()
                e_re = er[:, j].unsqueeze(1).to_broadcast([P, 2, CH])
                e_im = ei[:, j].unsqueeze(1).to_broadcast([P, 2, CH])
                two = lambda t: t.rearrange("p (a c) -> p a c", a=2)
                if j:
                    dve.wait_ge(hst_ready, j)
                for n, (a, b) in enumerate(((gr, e_re), (gi, e_im), (gr, e_im), (gi, e_re))):
                    ins = V.tensor_tensor(two(prod[:, n]), two(a), b, ALU.mult)
                    chain[0] += 1
                    ins.then_inc(dve_chain, 1)
                settle()
                V.memset(stat[:, 52:53], 0.0).then_inc(prod_ready, 1)

            def exponents(h):
                if h == 0:
                    dve.wait_ge(hst_ready, SJ)
                    dve.wait_ge(mb_evac, 5)
                if h == 2:
                    dve.wait_ge(ys_done, SJ)
                for jb in range(NT):
                    note(V.tensor_scalar(wgt[:, h, WBLK[jb]:WBLK[jb + 1]], mbc[:, h, P * jb:SEQ],
                                         cols[:, 4 * jb + h:4 * jb + h + 1], 0.0, ALU.subtract, ALU.max))
                note(V.tensor_scalar(wgt[0:TS, h, WBLK[NT]:], mbc[0:TS, h, LAST:T], cols[0:TS, 52 + h:53 + h], 0.0,
                                     ALU.subtract, ALU.max))
                settle()
                V.memset(stat[:, 52:53], 0.0).then_inc(d_ready, 1)

            def conv_in(c):
                if c == 0:
                    note(V.memset(zp[:, :, 0:2], 0.0))
                    note(V.tensor_copy(zs[:, :, :, 0:2], conv0))
                note(V.tensor_tensor(zp[:, c, 2:], cg[:, c, 0:SEQ], act_t[:, c, 0:SEQ], ALU.mult))
                note(V.tensor_tensor(zs[:, c, :, 2:], cg[:, c, SEQ:].rearrange("p (b t) -> p b t", b=DEC_BATCH),
                                     act_t[:, c, SEQ:].rearrange("p (b t) -> p b t", b=DEC_BATCH), ALU.mult))
                settle()
                w = prm_["conv_w"].rearrange("p (w c) -> p w c", c=2)
                o_p = cg[:, c, 0:SEQ]
                o_s = cg[:, c, SEQ:].rearrange("p (b t) -> p b t", b=DEC_BATCH)
                note(V.tensor_scalar(o_p, zp[:, c, 0:SEQ], w[:, 0, c:c + 1], None, ALU.mult))
                note(V.tensor_scalar(o_s, zs[:, c, :, 0:DEC_SEQ], w[:, 0, c:c + 1], None, ALU.mult))
                for n in range(1, CONV_W):
                    settle()
                    note(V.scalar_tensor_tensor(o_p, zp[:, c, n:n + SEQ], w[:, n, c:c + 1], o_p, ALU.mult, ALU.add))
                    note(V.scalar_tensor_tensor(o_s, zs[:, c, :, n:n + DEC_SEQ], w[:, n, c:c + 1], o_s, ALU.mult, ALU.add))
                settle()
                V.memset(stat[:, 53:54], 0.0).then_inc(conv_used, 1)

            def conv_out(c):
                note(V.tensor_tensor(cg[:, c], cg[:, c], act_t[:, c], ALU.mult))
                settle()
                V.memset(stat[:, 53:54], 0.0).then_inc(conv_used, 1)
                V.memset(stat[:, 54:55], 0.0).then_inc(outc_ready, 1)

            for s in range(2, M_END + 2):
                u = MIX_BASE + s
                lo_part(u, u % 2)
                if s == 2:
                    token_scale(7, D_MODEL, 16)
                    cnt["bc"] += 1
                if s == 3:
                    evac(0)
                if s >= 3:
                    evac(s - 2)
                gate(s)
                if s - 1 in S5_STEP:
                    s5_scan(S5_STEP.index(s - 1))
                if s in S5_STEP:
                    s5_in(S5_STEP.index(s))
                if s == 21:
                    exponents(0)
                    exponents(1)
                if s == 22:
                    dve.wait_ge(ys_done, SJ)
                    dve.wait_ge(yss_done, 1)
                    for c in range(2):
                        d = prm_["s5_d"][:, c:c + 1]
                        note(V.scalar_tensor_tensor(gl[:, c, 0:SEQ], ut[:, c, 0:SEQ], d, ps[:, 6 + c, :], ALU.mult, ALU.add))
                        note(V.scalar_tensor_tensor(gl[:, c, SEQ:], ut[:, c, SEQ:], d, ps[:, 4, c * TS:(c + 1) * TS],
                                                    ALU.mult, ALU.add))
                    settle()
                    V.memset(stat[:, 52:53], 0.0).then_inc(ys_evac, 1)
                    exponents(2)
                    exponents(3)
                if s in (M_HC + 2, M_HC + 3):
                    conv_in(s - M_HC - 2)
                if s in (M_BG + 2, M_BG + 3):
                    conv_out(s - M_BG - 2)

            for m in range(2):
                dve.wait_ge(glu_sig, 2)
                V.tensor_tensor(gl[:, m], gl[:, m], act_t[:, m], ALU.mult).then_inc(outb_ready, 1)

            def cat_tile(src, kk, bank, g, sample_at=8):
                def write(out):
                    V.scalar_tensor_tensor(out[:, 0:SEQ], src[:, 0:SEQ], g, ps[:, bank, :], ALU.mult, ALU.mult).then_inc(dve_chain, 1)
                    chain[0] += 1
                    V.scalar_tensor_tensor(out[:, SEQ:T], src[:, SEQ:T], g, ps[:, 6, sample_at:sample_at + TS], ALU.mult, ALU.mult)\
                     .then_inc(dve_chain, 1)
                    chain[0] += 1
                    settle()
                    V.memset(stat[:, 55:56], 0.0).then_inc(xf_ready, 1)
                return (kk, write)

            mix_g = prm_["mix_g"]
            for n in range(2):
                dve.wait_ge(xsq_ready, 2 * KD + 2 * n + 2)
                V.tensor_tensor(dve_t[:, n], act_t[:, 0], act_t[:, 1], ALU.add).then_inc(xsq_used, 2)
            def sample_q(h):
                if h == 0:
                    link(V.memset(prodn[:], 0.0))
                else:
                    dve.wait_ge(num_done, h)
                bt = lambda t: t.rearrange("p (b t) -> p b t", b=DEC_BATCH)
                link(V.tensor_tensor(qs[:], q[:, h, SEQ:], sbc[:, h], ALU.mult))
                V.tensor_tensor(bt(prodn[:, P - TS:]), bt(qs[:]), n0[:, h].unsqueeze(2).to_broadcast([P, DEC_BATCH, DEC_SEQ]),
                                ALU.mult).then_inc(qs_ready, 1)

            def add_memory(h, half):
                b0 = half * 4
                dve.wait_ge(cdec_ready, h + 1)
                dve.wait_ge(cps_done, 2 * h + half + 1)
                dst = cs[:, h, b0:b0 + 4]
                V.tensor_tensor(dst, ps[:, 7, :].rearrange("p (b d) -> p b d", b=4), dst, ALU.add).then_inc(cps_used, 1)

            def weighted(h):
                dve.wait_ge(sc_done, h + 1)
                dve.wait_ge(w_ready, h + 1)
                for a, b, c0 in ((0, 512, 0), (512, 896, 512), (896, WBLK[NT], 1024)):
                    note(V.tensor_tensor(wgt[:, h, a:b], psf[:, c0:c0 + b - a], wgt[:, h, a:b], ALU.mult))
                note(V.tensor_tensor(wgt[0:TS, h, WBLK[NT]:], ps[0:TS, 1, 384:512], wgt[0:TS, h, WBLK[NT]:], ALU.mult))
                settle()
                V.memset(stat[:, 52:53], 0.0).then_inc(p_ready, 1)

            weighted(0)
            sample_q(0)
            scale_col(6, D_CONV, 2)
            scaled([cat_tile(cg[:, c], c, 0, mix_g[:, c:c + 1], 32) for c in range(2)] +
                   [cat_tile(gl[:, c], 2 + c, 1, mix_g[:, 2 + c:3 + c], 64) for c in range(2)])

            for h in range(MH + 1):
                if 0 < h < MH:
                    weighted(h)
                if h >= 1:
                    n = cnt["norm"]
                    cnt["norm"] += 1
                    dve.wait_ge(stat_done, n + 1)
                    link(V.tensor_tensor(stat[:, 0:NTT], ps[:, 6, 0:NTT], stat[:, 40:40 + NTT], ALU.mult))
                    V.tensor_scalar(stat[:, 0:NTT], stat[:, 0:NTT], 1.0 / DH, EPS, ALU.mult, ALU.add).then_inc(var_ready, 1)
                if h < MH:
                    add_memory(h, 0)
                if h >= 1:
                    dve.wait_ge(std_ready, n + 1)
                    link(V.reciprocal(stat[:, 16:16 + NTT], stat[:, 16:16 + NTT]))
                    V.tensor_tensor(stat[:, 16:16 + NTT], stat[:, 16:16 + NTT], stat[:, 32:32 + NTT], ALU.mult)\
                     .then_inc(rcol_ready, 1)
                if h < MH:
                    add_memory(h, 1)
                    dve.wait_ge(num_done, h + 1)
                    dve.wait_ge(o_ready, h + 1)
                    note(V.tensor_tensor(mbc[:, h, 0:SEQ], ps[:, 3 + h % 2, :], mbc[:, h, 0:SEQ], ALU.mult))
                    note(V.tensor_tensor(mbc[:, h, SEQ:], ps[:, 5, 0:TS], mbc[:, h, SEQ:], ALU.mult))
                    note(V.tensor_copy(stat[:, 24:24 + NTT], ps[:, 5, TS:TS + NTT]))
                    settle()
                    V.memset(stat[:, 52:53], 0.0).then_inc(hso_ready, 1)
                if h >= 1:
                    dve.wait_ge(bc_done, n + 1)
                    scaled([cat_tile(mbc[:, h - 1], 3 + h, 3 + (h - 1) % 2, mix_g[:, 3 + h:4 + h])])
                if h < MH:
                    link(V.scalar_tensor_tensor(stat[:, 24:24 + NTT], stat[:, 24:24 + NTT], -1.0, stat[:, 24:24 + NTT],
                                                ALU.mult, ALU.max))
                    link(V.tensor_tensor(stat[:, 24:24 + NTT], stat[:, 24:24 + NTT], cols[:, 32 + h:52:MH], ALU.max))
                    link(V.reciprocal(stat[:, 32:32 + NTT], stat[:, 24:24 + NTT]))
                    link(V.tensor_tensor(stat[:, 40:40 + NTT], stat[:, 32:32 + NTT], stat[:, 32:32 + NTT], ALU.mult))
                    dve.wait_ge(st_done, h + 1)
                    note(V.tensor_copy(pst[:, h], ps[:, 7, 0:P + 1]))
                    note(V.tensor_tensor(nst[:, h], n0[:, h], sbc[:, h, DEC_SEQ - 1::DEC_SEQ], ALU.mult))
                    settle()
                    link(V.tensor_tensor(nst[:, h], nst[:, h], ps[:, 7, P + 8:P + 8 + DEC_BATCH], ALU.add))
                    V.memset(stat[:, 52:53], 0.0).then_inc(st_evac, 1)
                    if h < MH - 1:
                        sample_q(h + 1)

            link(V.memset(acc[:], 0.0))
            def out_evac(m):
                dve.wait_ge(unit_used, OUT_BASE + m + 3)
                V.tensor_copy(halves(y[:, m]), pair(2 * (m % 2))).then_inc(y_evac, 1)
                dve.wait_ge(ysq_ready, KD + m + 1)
                dve.wait_ge(ysq_used, KD + m + 2)
                V.tensor_tensor(acc[:], acc[:], act_t[:, m % 2], ALU.add).then_inc(ysq_used, 1)

            for m in range(2, KD):
                u = OUT_BASE + m
                lo_part(u, u % 2)
                out_evac(m - 2)

            def ffn2_inputs():
                post_norm(1, lambda: scale_col(6, D_MODEL), lambda kk: input_lo(4, kk))

            tail = ffn(1, FFN2_BASE, FT, 32, 2 * KD, [lambda: out_evac(6), lambda: out_evac(7)], ffn2_inputs)
            tail[0]()
            tail[1]()
            post_norm(2, lambda: ffn_scale(6))

        @block.gpsimd
        def _(pool):
            G = nc.gpsimd
            chain = [0]

            def link(ins):
                chain[0] += 1
                ins.then_inc(pool_chain, 1)
                pool.wait_ge(pool_chain, chain[0])

            def note(ins):
                chain[0] += 1
                ins.then_inc(pool_chain, 1)

            def settle():
                pool.wait_ge(pool_chain, chain[0])

            def signal(s_):
                settle()
                G.memset(stat[:, 61:62], 0.0).then_inc(s_, 1)

            def par(r):
                return s5p[:, r, :]

            def madd(out, src, a, b):
                return G.tensor_scalar(out, src, a, b, ALU.mult, ALU.add)

            def sum_squares():
                n = sum_squares.tiles
                pool.wait_ge(xsq_ready, n + 2)
                G.tensor_tensor(acc[:], act_t[:, n % 2], act_t[:, (n + 1) % 2], ALU.add).then_inc(xsq_used, 2)
                for kk in range(2, KD):
                    pool.wait_ge(xsq_ready, n + kk + 1)
                    pool.wait_ge(xsq_used, n + kk)
                    G.tensor_tensor(acc[:], acc[:], act_t[:, (n + kk) % 2], ALU.add).then_inc(xsq_used, 1)
                pool.wait_ge(xsq_used, n + KD)
                G.memset(stat[:, 61:62], 0.0).then_inc(xacc_ready, 1)
            sum_squares.tiles = 0
            sum_squares()

            pool.wait_ge(prm_in, 32)
            pool.wait_ge(s5_par, 1)
            tp = tpos
            for j in range(SJ):
                turns, whole, rest, small = (ang[:, n] for n in range(4))
                note(madd(turns, tp, s5p[:, FF, j:j + 1], MAGIC))
                note(madd(rest, tp, s5p[:, FHI, j:j + 1], 0.0))
                note(madd(small, tp, s5p[:, FLO, j:j + 1], 0.0))
                settle()
                link(G.tensor_scalar(whole, turns, -MAGIC, 1.0, ALU.add, ALU.mult))
                link(G.tensor_tensor(rest, rest, whole, ALU.subtract))
                link(G.tensor_tensor(rest, rest, small, ALU.add))
                link(madd(turns, rest, 1.0, MAGIC))
                link(G.tensor_scalar(whole, turns, -MAGIC, 1.0, ALU.add, ALU.mult))
                link(G.tensor_tensor(angd[:, j], rest, whole, ALU.subtract))
                signal(ang_ready)
            for j in range(SJ):
                pool.wait_ge(e_sin, 3 * j + 3)
                note(madd(er[:, j], er[:, j], -2.0, 1.0))
            settle()
            lim = prm_["a_im"]
            note(G.tensor_tensor(par(AR), par(MAG), er[:, :, 0], ALU.mult))
            note(G.tensor_tensor(par(AI), par(MAG), ei[:, :, 0], ALU.mult))
            settle()
            link(G.tensor_scalar(par(S0), par(AR), -1.0, 1.0, ALU.add, ALU.mult))
            note(G.tensor_tensor(par(S1), par(S0), par(LRE), ALU.mult))
            note(G.tensor_tensor(par(S2), par(AI), lim, ALU.mult))
            note(G.tensor_tensor(par(S3), par(AI), par(LRE), ALU.mult))
            note(G.tensor_tensor(par(S4), par(S0), lim, ALU.mult))
            settle()
            note(G.tensor_tensor(par(S1), par(S1), par(S2), ALU.add))
            note(G.tensor_tensor(par(S3), par(S3), par(S4), ALU.subtract))
            settle()
            note(G.tensor_tensor(par(FRE), par(S1), par(IDEN), ALU.mult))
            note(G.tensor_tensor(par(FIM), par(S3), par(IDEN), ALU.mult))
            settle()
            fr = par(FRE).unsqueeze(2).to_broadcast([P, SJ, S5_CH])
            fi = par(FIM).unsqueeze(2).to_broadcast([P, SJ, S5_CH])
            cf = [ang[:, n, 0:P].rearrange("p (j c) -> p j c", j=SJ) for n in range(5)]
            note(G.tensor_tensor(cf[0], c_re, fr, ALU.mult))
            note(G.tensor_tensor(cf[1], c_im, fi, ALU.mult))
            note(G.tensor_tensor(cf[2], c_re, fi, ALU.mult))
            note(G.tensor_tensor(cf[3], c_im, fr, ALU.mult))
            settle()
            link(G.tensor_tensor(cf[4], cf[2], cf[3], ALU.add))
            for g in range(2):
                a, c = slice(64 * g, 64 * g + 64), slice(S5_CH * g, S5_CH * (g + 1))
                note(G.tensor_tensor(cbd[a, 0, :, c], cf[0][a], cf[1][a], ALU.subtract))
                note(madd(cbd[a, 1, :, c], cf[4][a], -1.0, 0.0))
                note(madd(cbd[a, 2, :, c], c_re[a], 1.0, 0.0))
                note(madd(cbd[a, 3, :, c], c_im[a], -1.0, 0.0))
            signal(f_ready)

            sum_squares.tiles = KD
            sum_squares()

            pool.wait_ge(x_new, KD)
            note(G.memset(row(R_KEEP), 1.0))
            note(G.memset(row(R_BND), BIG))
            settle()
            G.memset(starts(row(R_KEEP)), 0.0).then_inc(masks_ready, 2)
            G.memset(starts(row(R_BND)), -BIG).then_inc(masks_ready, 2)

            pool.wait_ge(bus_evac, 4)
            big = lambda r, n: par(r).unsqueeze(2).to_broadcast([P, SJ, n])
            note(G.tensor_tensor(tmp5[:, 0], bus[:, 0], big(FRE, TS), ALU.mult))
            note(G.tensor_tensor(tmp5[:, 1], bus[:, 1], big(FIM, TS), ALU.mult))
            note(G.tensor_tensor(tmp5[:, 2], bus[:, 1], big(FRE, TS), ALU.mult))
            note(G.tensor_tensor(tmp5[:, 3], bus[:, 0], big(FIM, TS), ALU.mult))
            settle()
            note(G.tensor_tensor(xs5[:, 0], tmp5[:, 0], tmp5[:, 1], ALU.subtract))
            note(G.tensor_tensor(xs5[:, 1], tmp5[:, 2], tmp5[:, 3], ALU.add))
            settle()
            bt = lambda t: t.rearrange("p j (b t) -> p j b t", b=DEC_BATCH)
            now = [bt(hs[:, r]) for r in range(2)]
            inp = [bt(xs5[:, r]) for r in range(2)]
            t5 = [tmp5[:, n, :, 0:DEC_BATCH] for n in range(4)]
            for t in range(DEC_SEQ):
                hr, hi = (now[r][:, :, :, t - 1] if t else h0[:, r] for r in range(2))
                note(G.tensor_tensor(t5[0], hr, big(AR, DEC_BATCH), ALU.mult))
                note(G.tensor_tensor(t5[1], hi, big(AI, DEC_BATCH), ALU.mult))
                note(G.tensor_tensor(t5[2], hi, big(AR, DEC_BATCH), ALU.mult))
                note(G.tensor_tensor(t5[3], hr, big(AI, DEC_BATCH), ALU.mult))
                settle()
                note(G.tensor_tensor(t5[0], t5[0], t5[1], ALU.subtract))
                note(G.tensor_tensor(t5[2], t5[2], t5[3], ALU.add))
                settle()
                note(G.tensor_tensor(now[0][:, :, :, t], t5[0], inp[0][:, :, :, t], ALU.add))
                note(G.tensor_tensor(now[1][:, :, :, t], t5[2], inp[1][:, :, :, t], ALU.add))
                settle()
            signal(hs_ready)

            def turned(j):
                pool.wait_ge(rot_ready, 4 * j + 4)
                G.tensor_tensor(rot[:, 0], rot[:, 0], rot[:, 1], ALU.add).then_inc(xrot_ready, 1)
                G.tensor_tensor(rot[:, 2], rot[:, 2], rot[:, 3], ALU.subtract).then_inc(xrot_ready, 1)

            turned(0)
            for j in range(SJ):
                if j + 1 < SJ:
                    turned(j + 1)
                pool.wait_ge(prod_ready, j + 1)
                if j:
                    pool.wait_ge(ys_done, j)
                note(G.tensor_tensor(hst[:, 0], prod[:, 0], prod[:, 1], ALU.subtract))
                note(G.tensor_tensor(hst[:, 1], prod[:, 2], prod[:, 3], ALU.add))
                settle()
                link(madd(hlast[:, :, j:j + 1], hst[:, :, SEQ - 1:SEQ], 1.0, 0.0))
                G.memset(stat[:, 61:62], 0.0).then_inc(hst_ready, 1)
            hr, hi = hlast[:, 0], hlast[:, 1]
            note(G.tensor_tensor(par(S0), hr, par(FRE), ALU.mult))
            note(G.tensor_tensor(par(S1), hi, par(FIM), ALU.mult))
            note(G.tensor_tensor(par(S2), hi, par(FRE), ALU.mult))
            note(G.tensor_tensor(par(S3), hr, par(FIM), ALU.mult))
            settle()
            note(G.tensor_tensor(s5o[:, 0], par(S0), par(S1), ALU.subtract))
            note(G.tensor_tensor(s5o[:, 1], par(S2), par(S3), ALU.add))
            for r in range(2):
                note(madd(s5so[:, r], now[r][:, :, :, DEC_SEQ - 1], 1.0, 0.0))
            signal(s5_out)

            for h in range(MH):
                note(madd(wkm[0:TS, h], cst_["batch"][0:TS], cols[0:TS, 56 + h:57 + h], 0.0))
            for h in range(MH):
                pool.wait_ge(w_exp, 2 * h + 2)
                for jb in range(NT):
                    w = wgt[:, h, WBLK[jb]:WBLK[jb] + P]
                    note(G.tensor_tensor(w, w, cst_["tri"], ALU.mult))
                w = wgt[0:TS, h, WBLK[NT]:]
                note(G.tensor_tensor(w, w, cst_["bmask"][0:TS], ALU.mult))
                signal(w_ready)
            for h in range(MH):
                pool.wait_ge(nat_evac, 2 * MH + 2)
                if h >= 2:
                    pool.wait_ge(st_done, h - 1)
                for a in range(NT):
                    note(madd(vw[:, h % 2, a, 0:P], vn[:, h, a], cols[:, 16 + 4 * a + h:17 + 4 * a + h], 0.0))
                note(madd(vw[:, h % 2, :, P], cols[:, 16 + h:32:MH], 1.0, 0.0))
                if h:
                    pool.wait_ge(cps_done, 2 * h)
                note(G.tensor_tensor(vbig[0:TS], sn[0:TS, 1, h].unsqueeze(1).to_broadcast([TS, DEC_BATCH, P]),
                                     wkm[0:TS, h].unsqueeze(2).to_broadcast([TS, DEC_BATCH, P]), ALU.mult))
                signal(vw_ready)
                pool.wait_ge(inter_done, h + 1)
                note(G.tensor_tensor(cs[:, h], cs[:, h],
                                     sbc[:, h, DEC_SEQ - 1::DEC_SEQ].unsqueeze(2).to_broadcast([P, DEC_BATCH, P]), ALU.mult))
                signal(cdec_ready)
            sum_squares.tiles = 2 * KD + 4 + MH
            sum_squares()

        @block.tensor
        def _(pe):
            mm = nc.tensor.matmul
            cnt = {"norm": 0, "sq": 0, "post": 0, "bc": 0, "acc": 0}

            def unit(par, bank, n, a_hi, a_lo, wait_k=None):
                for kk in range(n):
                    if wait_k:
                        wait_k(kk)
                    for i, (w, a) in enumerate(((wh, a_hi), (wh, a_lo), (wl, a_hi))):
                        for s in range(2):
                            last = mm(ps[:, bank + s, 0:HALF], w[par][:, kk * P:(kk + 1) * P],
                                      a[:, kk, s * HALF:(s + 1) * HALF], start=(kk == 0 and i == 0),
                                      stop=(kk == n - 1 and i == 2))
                last.then_inc(unit_used, 1)

            def ffn(u0, hb, yb, e0):
                def up(u, h, c, wait_k=None):
                    pe.wait_ge(split_done, u + c + 3)
                    if c % 2 == 0:
                        pe.wait_ge(h_ready, h + c // 2 + 1)
                    unit((u0 + c) % 2, 2 * c, KD, xh, xl, wait_k)

                for p, n in enumerate(PARTS):
                    if p == 0:
                        up(u0, hb, 0, lambda kk: pe.wait_ge(xl_ready, e0 + kk + 1))
                        up(u0, hb, 1)
                        input_sums(7)
                        up(u0, hb, 2)
                        spread(R_IN, 6, 7, 0).then_inc(bc_done, 1)
                        cnt["bc"] += 1
                        pe.wait_ge(bc_evac, cnt["bc"])
                        up(u0, hb, 3)
                    with pe.Fori(1 if p == 0 else 0, n // 2) as i:
                        for c in range(4):
                            if c < 2 and p:
                                pe.wait_ge(y_evac, yb + 1 + c)
                            up(u0 + 4 * i, hb + 2 * i, c)
                    u0 += 2 * n
                    with pe.Fori(0, KD // 2) as i:
                        for c in range(2):
                            pe.wait_ge(split_done, u0 + 2 * i + c + 3)
                            pe.wait_ge(y_evac, yb + 2 * i + c + 1)
                            unit((u0 + c) % 2, 2 * c, n, hh, hl,
                                 (lambda kk: pe.wait_ge(h_lo, hb + kk + 1)) if c == 0 else None)
                    u0 += KD
                    hb += n
                    yb += KD

            def token_sums(src, bank, first, last, at=0):
                for c in range(NTT):
                    lo = P * c if c < NT else LAST
                    ins = mm(ps[:, bank, at + c:at + c + 1], src[:, lo:lo + P], ones, start=(first and c == 0), stop=last,
                             skip_group_check=True)
                return ins

            def squares(i, n, bank):
                pe.wait_ge(xsq_ready, cnt["sq"] + 1)
                token_sums(act_t[:, cnt["sq"] % 2], bank, i == 0, i == n - 1).then_inc(xsq_used, 1)
                cnt["sq"] += 1
                if i == n - 1:
                    mm(ps[:, bank, NTT:NTT + 1], ident, ones, start=False, stop=True, skip_group_check=True)\
                        .then_inc(stat_done, 1)

            def spread(col, bank, bank_s, col_s, more=False):
                if not more:
                    cnt["norm"] += 1
                    pe.wait_ge(rcol_ready, cnt["norm"])
                for c in range(NTT):
                    w = P if c < NT else TS
                    out = ps[:, bank, P * c:P * c + P] if c < NT else ps[:, bank_s, col_s:col_s + TS]
                    ins = mm(out, stat[:, col + c:col + 1 + c].to_broadcast([P, P]), ident[:, P - w:P], start=True, stop=True)
                return ins

            def input_sums(bank):
                cnt["acc"] += 1
                pe.wait_ge(xacc_ready, cnt["acc"])
                token_sums(acc, bank, True, True).then_inc(stat_done, 1)
                cnt["sq"] += KD

            def post_norm():
                cnt["post"] += KD
                pe.wait_ge(ysq_used, cnt["post"] + 2)
                token_sums(acc, 6, True, True).then_inc(stat_done, 1)
                spread(16, 4, 5, 0).then_inc(bc_done, 1)

            pe.wait_ge(cst_in, 16)
            ffn(0, 0, 0, 0)
            post_norm()

            def gate_spread():
                pe.wait_ge(gv, 14)
                pe.wait_ge(ga, 6)
                pe.wait_ge(bus_evac, 4)
                for h in range(MH):
                    ins = mm(ps[:, 4 + h, :], sel[0:MH, h * P:(h + 1) * P], row(R_M, 0, SEQ), start=True, stop=True)
                ins.then_inc(mb_done, 1)

            def gate_turn():
                pe.wait_ge(mb_evac, 1)
                for r, src in enumerate((R_M, R_F)):
                    for h in range(MH):
                        at = (r * MH + h) * TS
                        mm(ps[:, 4, at:at + TS], sel[0:MH, h * P:(h + 1) * P], row(src, SEQ), start=True, stop=True)
                i4 = ident[0:MH, 0:MH]
                for n, r in enumerate((R_G, R_GM)):
                    for a in range(NT):
                        nc.tensor.transpose(ps[:, 5, 16 * n + 4 * a:16 * n + 4 * a + 4], row(r, P * a, P * a + P), i4)
                    nc.tensor.transpose(ps[0:TS, 5, 52 + 4 * n:56 + 4 * n], row(r, SEQ), i4)
                for a in range(NTT):
                    lo = P * a if a < NT else LAST
                    ins = nc.tensor.transpose(ps[:, 5, 32 + 4 * a:36 + 4 * a], row(R_B, lo, lo + P), i4)
                ins.then_inc(mb_done, 1)

            def sample_bu():
                pe.wait_ge(t_evac, M_U + 2)
                for r, mat in enumerate(("re", "im")):
                    for j in range(SJ):
                        a = slice(32 * (j % 4), 32 * (j % 4) + 32)
                        at = (2 * r + j // 4) * TS
                        ins = mm(ps[:, 4 + j % 4, at:at + TS], bbd[mat][a, j // 4, :], ut[a, j // 4, SEQ:], start=True, stop=True)
                ins.then_inc(bu_s, 1)

            def bu(j):
                if j == 0:
                    pe.wait_ge(mb_evac, 5)
                else:
                    pe.wait_ge(rot_ready, 4 * j)
                a = slice(32 * (j % 4), 32 * (j % 4) + 32)
                for bank, mat in ((4, "re"), (5, "im")):
                    ins = mm(ps[:, bank, :], bbd[mat][a, j // 4, :], ut[a, j // 4, 0:SEQ], start=True, stop=True)
                ins.then_inc(bu_done, 1)

            def s5_y(j):
                pe.wait_ge(hst_ready, j + 1)
                a = slice(32 * (j % 4), 32 * (j % 4) + 32)
                for r in range(2):
                    ins = mm(ps[a, 6 + j // 4, :], cbd[:, r, j, :], hst[:, r], start=(r == 0), stop=(r == 1))
                ins.then_inc(ys_done, 1)

            def s5_y_sample():
                pe.wait_ge(hs_ready, 1)
                pe.wait_ge(rot_ready, 4 * SJ)
                for j in range(SJ):
                    a = slice(32 * (j % 4), 32 * (j % 4) + 32)
                    for r in range(2):
                        ins = mm(ps[a, 4, (j // 4) * TS:(j // 4 + 1) * TS], cbd[:, 2 + r, j, :], hs[:, r, j],
                                 start=(r == 0), stop=(r == 1))
                ins.then_inc(yss_done, 1)

            def turn(h):
                pe.wait_ge(ys_evac, 1)
                if h:
                    pe.wait_ge(nat_evac, 2 * h)
                for a in range(NT):
                    nc.tensor.transpose(ps[:, 4, a * P:(a + 1) * P], k[:, h, a * P:(a + 1) * P], ident)
                for a in range(NT):
                    ins = nc.tensor.transpose(ps[:, 5, a * P:(a + 1) * P], v[:, h, a * P:(a + 1) * P], ident)
                ins.then_inc(nat_done, 1)

            after = {4: [sample_bu], 6: [gate_spread], 7: [gate_turn], 21: [lambda: s5_y_sample()],
                     22: [lambda: turn(0)], 23: [lambda: turn(1)], 24: [lambda: turn(2)]}
            for j in range(SJ):
                after.setdefault(S5_STEP[j] - 2, []).append(lambda j=j: bu(j))
                after.setdefault(S5_STEP[j] + 1, []).append(lambda j=j: s5_y(j))
            for i in range(M_END):
                u = MIX_BASE + i
                pe.wait_ge(split_done, u + 3)
                if i > 2:
                    pe.wait_ge(t_evac, i - 1)
                if i == 2:
                    input_sums(7)
                    unit(u % 2, 4, KD, xh, xl, lambda kk: spread(16, 6, 7, 0).then_inc(bc_done, 1) if kk == 3 else None)
                else:
                    unit(u % 2, 2 * (i % 2), KD, xh, xl, (lambda kk: pe.wait_ge(xl_ready, KD + kk + 1)) if i == 0 else None)
                for f in after.get(i, ()):
                    f()

            pe.wait_ge(gelu_ready, 1)
            for m in range(2):
                if m == 1:
                    turn(3)
                    pe.wait_ge(nat_evac, 2 * MH)
                bank = 6 if m == 0 else 4
                wg = prm_["w_glu"].rearrange("p (k c) -> p k c", k=2)
                for kk in range(2):
                    for s in range(2):
                        ins = mm(ps[:, bank + s, 0:HALF], wg[:, kk, m * P:(m + 1) * P], gl[:, kk, s * HALF:(s + 1) * HALF],
                                 start=(kk == 0), stop=(kk == 1))
                ins.then_inc(glu_done, 1)
            pe.wait_ge(glu_sig, 1)
            for h in range(MH):
                nc.tensor.transpose(ps[0:TS, 6, h * P:(h + 1) * P], k[:, h, SEQ:], ident)
            for h in range(MH):
                ins = nc.tensor.transpose(ps[0:TS, 7, h * P:(h + 1) * P], v[:, h, SEQ:], ident)
            ins.then_inc(nat_done, 1)

            def scores(h):
                if h:
                    pe.wait_ge(p_ready, h)
                for jb in range(NT):
                    at = (0, 512, 1024, 1280)[jb]
                    mm(psf[:, at:at + SEQ - P * jb], k[:, h, P * jb:P * jb + P], q[:, h, P * jb:SEQ], start=True, stop=True)
                mm(ps[0:TS, 1, 384:512], k[:, h, SEQ:], q[:, h, LAST:T], start=True, stop=True).then_inc(sc_done, 1)

            pe.wait_ge(t_evac, M_END)
            scores(0)
            pe.wait_ge(glu_sig, 2)
            pe.wait_ge(nat_evac, 2 * MH + 2)
            for n in range(2):
                cnt["sq"] += 2
                pe.wait_ge(xsq_used, cnt["sq"])
                ins = token_sums(dve_t[:, n], 6, n == 0, True, 8 * n)
            ins.then_inc(stat_done, 1)
            pe.wait_ge(p_ready, 1)
            spread(16, 0, 6, 32)
            spread(24, 1, 6, 64, more=True).then_inc(bc_done, 1)

            pe.wait_ge(cs_in, 16)
            for h in range(MH + 1):
                if h < MH:
                    if h:
                        pe.wait_ge(hso_ready, h)
                    pe.wait_ge(qs_ready, h + 1)
                    for b in range(DEC_BATCH):
                        c = slice(b * DEC_SEQ, (b + 1) * DEC_SEQ)
                        ins = mm(ps[:, 5, c], cs[:, h, b], qs[:, c], start=(b == 0), stop=False, skip_group_check=True)
                    ins.then_inc(inter_done, 1)
                    if h:
                        pe.wait_ge(st_evac, h)
                    pe.wait_ge(vw_ready, h + 1)
                    mm(ps[:, 7, :], sn[0:TS, 0, h], vbig[0:TS, 0:4].rearrange("p b d -> p (b d)"), start=True, stop=True)\
                        .then_inc(cps_done, 1)
                if h:
                    pe.wait_ge(xf_ready, 4 + h - 1)
                    squares(0, 1, 6)
                if h < MH:
                    pe.wait_ge(cps_used, 2 * h + 1)
                    mm(ps[:, 7, :], sn[0:TS, 0, h], vbig[0:TS, 4:8].rearrange("p b d -> p (b d)"), start=True, stop=True)\
                        .then_inc(cps_done, 1)
                    pe.wait_ge(p_ready, h + 1)
                    if h > 1:
                        pe.wait_ge(xf_ready, 4 + h - 1)
                    for jb in range(NT):
                        mm(ps[:, 3 + h % 2, P * jb:], vn[:, h, jb], wgt[:, h, WBLK[jb]:WBLK[jb + 1]], start=(jb == 0),
                           stop=(jb == NT - 1), skip_group_check=True)
                    own = wgt[0:TS, h, WBLK[NT]:]
                    mm(ps[:, 5, 0:TS], sn[0:TS, 1, h], own[:, P - TS:], start=False, stop=True, skip_group_check=True)
                    for a in range(NT):
                        for jb in range(a + 1):
                            at = WBLK[jb] + P * (a - jb)
                            mm(ps[:, 5, TS + a:TS + a + 1], wgt[:, h, at:at + P], ones, start=False, stop=(jb == a),
                               skip_group_check=True)
                    mm(ps[:, 5, TS + NT:TS + NTT], own, ones[0:TS], start=False, stop=False, skip_group_check=True)
                    mm(ps[:, 5, TS + NT:TS + NTT], prodn[:], ones, start=False, stop=True, skip_group_check=True)\
                        .then_inc(num_done, 1)
                if h:
                    spread(16, 3 + (h - 1) % 2, 6, 8).then_inc(bc_done, 1)
                if h < MH:
                    pe.wait_ge(cps_used, 2 * h + 2)
                    for a in range(NT):
                        mm(ps[:, 7, 0:P + 1], kn[:, h, a], vw[:, h % 2, a], start=(a == 0), stop=(a == NT - 1))
                    mm(ps[:, 7, P + 8:P + 8 + DEC_BATCH], sn[0:TS, 0, h], wkm[0:TS, h], start=True, stop=True)\
                        .then_inc(st_done, 1)
                    if h == 0:
                        pe.wait_ge(xf_ready, 4)
                    if h < MH - 1:
                        scores(h + 1)

            for m in range(KD):
                u = OUT_BASE + m
                pe.wait_ge(split_done, u + 3)
                if m == 0:
                    pe.wait_ge(xf_ready, KD)
                pe.wait_ge(y_evac, 24 + m + 1)
                unit(u % 2, 2 * (m % 2), KD, xh, xl, (lambda kk: pe.wait_ge(xl_ready, 2 * KD + kk + 1)) if m == 0 else None)
            post_norm()
            cnt["bc"] += 1
            ffn(FFN2_BASE, FT, 32, 3 * KD)
            post_norm()


def _tiles(w, rows, cols):
    return w.reshape(rows, P, cols, P).transpose(2, 1, 0, 3).reshape(cols, P, rows * P)


def _features(a):
    n = a.shape[-1] // P
    a = a.reshape(a.shape[:-1] + (n, P))
    return np.moveaxis(np.moveaxis(a, -1, 0), -1, 1)


_OUTS = {
    "o_yT": (P, KD, T), "o_pC": (P, MH, P + 1), "o_m": (MH, 1 + TS), "o_ps5": (P, 2, SJ), "o_pconv": (P, 2, 2),
    "o_sC": (P, MH, DEC_BATCH, P), "o_sn": (P, MH, DEC_BATCH), "o_ss5": (P, 2, SJ, DEC_BATCH),
    "o_sconv": (P, 2, DEC_BATCH, 2),
}


def _constants():
    c = np.zeros((P, NCST), np.float32)
    put = lambda n, a: c.__setitem__((slice(0, a.shape[0]), slice(*CST[n])), a)
    put("ident", np.eye(P, dtype=np.float32))
    put("ones", np.ones((P, 1), np.float32))
    put("tri", np.triu(np.ones((P, P), np.float32)))
    bm = np.zeros((TS, P), np.float32)
    for b in range(DEC_BATCH):
        a = b * DEC_SEQ
        bm[a:a + DEC_SEQ, P - TS + a:P - TS + a + DEC_SEQ] = np.triu(np.ones((DEC_SEQ, DEC_SEQ), np.float32))
    put("bmask", bm)
    put("batch", np.repeat(np.eye(DEC_BATCH, dtype=np.float32), DEC_SEQ, axis=0))
    c2 = np.zeros((P, NCST2), np.float32)
    c2[0:MH, 0:MH * P] = np.repeat(np.eye(MH, dtype=np.float32), P, axis=1)
    c2[:, MH * P:] = np.arange(1, CH + 1, dtype=np.float32)
    return c, c2


def _layout(i):
    g = lambda n: np.asarray(i[n])[0]
    out = {}
    xs = np.concatenate([np.asarray(i["x_prompt"])[0], np.asarray(i["x_sample"]).reshape(TS, D_MODEL)])
    out["xT"] = _features(xs)
    for f in range(2):
        w1, w3, w2 = (g(f"ffn{f + 1}_{w}") for w in ("w1", "w3", "w2"))
        out[f"w13_{f}"] = np.stack([_tiles(w1, KD, FT), _tiles(w3, KD, FT)], axis=1).reshape(2 * FT, P, UNIT)
        out[f"w2_{f}"] = _tiles(w2, FT, KD)
    w = g("w_in")
    dm = MH * DH
    at = np.cumsum([0, dm, dm, dm, dm, MH, MH, 256, 256, 256, 256])
    q_, k_, v_, o_, i_, f_, u_, b_, c_, h_ = (w[:, a:b] for a, b in zip(at[:-1], at[1:]))
    gate = np.zeros((D_MODEL, P), w.dtype)
    gate[:, 0:MH] = i_
    gate[:, 32:32 + MH] = f_
    out["win"] = _tiles(np.concatenate([gate, u_, q_, k_, v_, c_, h_, b_, o_], axis=1), KD, M_END)
    order = lambda a: np.concatenate([a[768:1024], a[512:768], a[0:512]])
    out["wout"] = _tiles(order(g("w_out")), KD, KD)
    prm = np.zeros((P, NPRM), np.float32)

    def put(n, a):
        prm[0:a.shape[0], slice(*PRM[n])] = a.reshape(a.shape[0], -1)

    put("norm_g", np.moveaxis(_features(g("norm_g")), 1, 2))
    put("mix_g", _features(order(g("mix_g"))))
    put("conv_w", np.moveaxis(_features(g("conv_w")), 1, 2))
    put("s5_d", _features(g("s5_d")))
    states = lambda a: np.moveaxis(a.reshape((SJ, P) + a.shape[2:]), 0, 1)
    put("a_re", states(g("s5_a_re")))
    put("a_im", states(g("s5_a_im")))
    put("log_dt", states(np.repeat(g("s5_log_dt")[:, None], S5_P, axis=1)))
    put("gate_b", np.stack([g("ig_bias"), g("fg_bias")], axis=1))
    put("m0", g("state_mlstm_m").T)
    put("h0", np.stack([states(np.moveaxis(g(n), 0, -1)) for n in ("state_s5_re", "state_s5_im")], axis=1))
    put("conv0", _features(g("state_conv")))
    put("n0", g("state_mlstm_n").transpose(2, 1, 0))
    for n in ("re", "im"):
        put(f"c_{n}", states(g(f"s5_c_{n}").transpose(0, 2, 1)))
        b = g(f"s5_b_{n}").transpose(0, 2, 1).reshape(2, 4, 2, S5_CH, S5_P)
        bd = np.zeros((2, 4, 2, S5_CH, 2, S5_P), b.dtype)
        for gg in range(2):
            bd[:, :, gg, :, gg] = b[:, :, gg]
        put(f"b_{n}", np.moveaxis(bd.reshape(2, P, P), 0, 1))
    put("w_glu", np.moveaxis(g("w_glu").reshape(2, P, 256), 0, 1))
    out["prm"] = prm
    out["cst"], out["cst2"] = _constants()
    out["cT"] = g("state_mlstm_C").transpose(3, 1, 0, 2)
    return {n: np.ascontiguousarray(a) for n, a in out.items()}


def kernel(**inputs):
    import concourse.bacc as bacc
    from concourse.bass_utils import run_bass_kernel_spmd as run

    arrays = _layout(inputs)
    nc = bacc.Bacc("TRN2", target_bir_lowering=False, num_devices=1)
    A = {n: nc.dram_tensor(n, a.shape, F32, kind="ExternalInput").ap() for n, a in arrays.items()}
    for n, shape in _OUTS.items():
        A[n] = nc.dram_tensor(n, shape, F32, kind="ExternalOutput").ap()
    build(nc, A)
    r = run(nc, [arrays], core_ids=[0]).results[0]
    o = {n: np.asarray(r[n]) for n in _OUTS}
    rows = lambda a: np.moveaxis(a, (0, 1), (-1, -2)).reshape(a.shape[2:] + (-1,))
    y = rows(o["o_yT"])
    state = lambda a: np.moveaxis(a, 1, 0).reshape((S5_G, S5_P) + a.shape[2:])
    return (
        y[None, :SEQ], y[SEQ:].reshape(DEC_BATCH, DEC_SEQ, D_MODEL),
        o["o_pC"][:, :, :P].transpose(1, 2, 0)[None, None], o["o_pC"][:, :, P].T[None, None],
        o["o_m"][:, 0][None, None], state(o["o_ps5"][:, 0])[None, None], state(o["o_ps5"][:, 1])[None, None],
        rows(o["o_pconv"])[None, None],
        o["o_sC"].transpose(2, 1, 3, 0)[None], o["o_sn"].transpose(2, 1, 0)[None], o["o_m"][:, DEC_SEQ::DEC_SEQ].T[None],
        np.moveaxis(state(o["o_ss5"][:, 0]), -1, 0)[None], np.moveaxis(state(o["o_ss5"][:, 1]), -1, 0)[None],
        rows(o["o_sconv"])[None],
    )
```
